# Optimizing a Trainium2 kernel written in Bass

```python
import jax
import jax.numpy as jnp
from jax import lax
import numpy as np

D_MODEL = 1024
BATCH = 1
SEQ = 2048
DEPTH = 1
DEC_BATCH = 8
DEC_SEQ = 8
PAST_LEN = 2048
PAGE_SIZE = 128

HEAD_DIM = 64
A_HEADS = 6
A_WIDTH = A_HEADS * HEAD_DIM
DILATED = ((128, 1), (512, 4), (2048, 16))
MAX_WINDOW = 2048
BAND_BLOCK = 128
LRU_BLOCKS = 6
LRU_BLOCK_DIM = 64
LRU_WIDTH = LRU_BLOCKS * LRU_BLOCK_DIM
CONV_W = 4
LRU_C = 8.0
C_HEADS = 6
C_KDIM = 128
C_VDIM = 64
C_KWIDTH = C_HEADS * C_KDIM
C_VWIDTH = C_HEADS * C_VDIM
C_CHUNK = 64
MIX_WIDTH = A_WIDTH + LRU_WIDTH + C_VWIDTH
SPLIT_SIZES = (A_WIDTH, A_WIDTH, A_WIDTH, A_WIDTH, LRU_WIDTH, LRU_WIDTH, C_KWIDTH, C_KWIDTH, C_VWIDTH, C_VWIDTH)
IN_WIDTH = sum(SPLIT_SIZES)
RMS_EPS = 1e-6

kernel_name = 'hybrid_dilated_rglru_hgrn2_step'

def rmsnorm(x, g):
    xf = x.astype(jnp.float32)
    y = xf * lax.rsqrt(jnp.mean(xf * xf, axis=-1, keepdims=True) + RMS_EPS)
    return (y * g.astype(jnp.float32)).astype(x.dtype)

def split_columns(z):
    parts, start = [], 0
    for size in SPLIT_SIZES:
        parts.append(z[..., start:start + size])
        start += size
    return parts

def dilated_branch_prompt(q, k, v, window, dilation):
    b, s, h, dh = q.shape
    n_back = window // dilation
    m = s // dilation
    nb = -(-m // BAND_BLOCK)
    mp = nb * BAND_BLOCK

    def to_blocks(t):
        t = t.reshape(b, m, dilation, h, dh).transpose(0, 2, 1, 3, 4)
        t = jnp.pad(t, ((0, 0), (0, 0), (0, mp - m), (0, 0), (0, 0)))
        return t.reshape(b, dilation, nb, BAND_BLOCK, h, dh)

    def band(t):
        prev = jnp.pad(t, ((0, 0), (0, 0), (1, 0), (0, 0), (0, 0), (0, 0)))[:, :, :-1]
        return jnp.concatenate([prev, t], axis=3)

    qb = to_blocks(q)
    kband = band(to_blocks(k))
    vband = band(to_blocks(v))
    scores = jnp.einsum('brnqhd,brnkhd->brnhqk', qb, kband,
                        preferred_element_type=jnp.float32) * (dh ** -0.5)
    qi = jnp.arange(BAND_BLOCK)[:, None]
    ki = jnp.arange(2 * BAND_BLOCK)[None, :]
    dist = BAND_BLOCK + qi - ki
    blk = jnp.arange(nb)[:, None, None]
    valid = (dist >= 0) & (dist <= n_back) & ((blk > 0) | (ki >= BAND_BLOCK))
    scores = jnp.where(valid[:, None], scores, -jnp.inf)
    mx = jnp.max(scores, axis=-1, keepdims=True)
    p = jnp.exp(scores - mx)
    l = jnp.sum(p, axis=-1, keepdims=True)
    o = jnp.einsum('brnhqk,brnkhd->brnqhd', p, vband.astype(jnp.float32)) / jnp.swapaxes(l, 3, 4)
    lse = jnp.swapaxes((mx + jnp.log(l))[..., 0], 3, 4)

    def from_blocks(t):
        t = t.reshape(b, dilation, mp, *t.shape[4:])[:, :, :m]
        t = jnp.moveaxis(t, 1, 2)
        return t.reshape(b, s, *t.shape[3:])

    return from_blocks(o), from_blocks(lse)

def dilated_branch_sample(q, k_all, v_all, window, dilation, n_buf):
    t_len, dh = q.shape[1], q.shape[-1]
    n_back = window // dilation
    idx = n_buf + jnp.arange(t_len)[:, None] - dilation * jnp.arange(n_back + 1)[None, :]
    valid = idx >= 0
    idx = jnp.maximum(idx, 0)
    kg = jnp.take(k_all, idx, axis=1)
    vg = jnp.take(v_all, idx, axis=1)
    scores = jnp.einsum('bthd,btnhd->bthn', q, kg, preferred_element_type=jnp.float32) * (dh ** -0.5)
    scores = jnp.where(valid[:, None, :], scores, -jnp.inf)
    mx = jnp.max(scores, axis=-1, keepdims=True)
    p = jnp.exp(scores - mx)
    l = jnp.sum(p, axis=-1, keepdims=True)
    o = jnp.einsum('bthn,btnhd->bthd', p, vg.astype(jnp.float32)) / l
    return o, (mx + jnp.log(l))[..., 0]

def combine_by_denominator(branches):
    outs = jnp.stack([o for o, _ in branches], axis=0)
    lses = jnp.stack([l for _, l in branches], axis=0)
    wts = jax.nn.softmax(lses, axis=0)
    return jnp.sum(wts[..., None] * outs, axis=0)

def causal_conv(x_pad, conv_w, conv_b):
    s = x_pad.shape[1] - (CONV_W - 1)
    out = conv_b
    for j in range(CONV_W):
        out = out + x_pad[:, j:j + s] * conv_w[j]
    return out

def rg_lru(xc, h0, w_a, b_a, w_x, b_x, lam):
    bsz, s, _ = xc.shape
    xb = xc.reshape(bsz, s, LRU_BLOCKS, LRU_BLOCK_DIM)
    r = jax.nn.sigmoid(jnp.einsum('bshi,hij->bshj', xb, w_a).reshape(bsz, s, LRU_WIDTH).astype(jnp.float32)
                       + b_a.astype(jnp.float32))
    i = jax.nn.sigmoid(jnp.einsum('bshi,hij->bshj', xb, w_x).reshape(bsz, s, LRU_WIDTH).astype(jnp.float32)
                       + b_x.astype(jnp.float32))
    log_a = -LRU_C * r * jax.nn.softplus(-lam.astype(jnp.float32))
    a = jnp.exp(log_a)
    u = jnp.sqrt(-jnp.expm1(2.0 * log_a)) * (i * xc.astype(jnp.float32))

    def combine(e1, e2):
        a1, b1 = e1
        a2, b2 = e2
        return a1 * a2, a2 * b1 + b2

    a_cum, u_cum = lax.associative_scan(combine, (a, u), axis=1)
    h = a_cum * h0.astype(jnp.float32)[:, None] + u_cum
    return h, h[:, -1]

def hgrn2(q, k, v, logf, s0):
    bsz, s = q.shape[:2]
    L = min(C_CHUNK, s)
    nc = -(-s // L)
    pad = nc * L - s

    def chunks(t):
        t = jnp.pad(t, ((0, 0), (0, pad), (0, 0), (0, 0)))
        return t.reshape(bsz, nc, L, *t.shape[2:]).transpose(1, 0, 3, 2, 4)

    qc, kc, vc, fc = chunks(q), chunks(k), chunks(v), chunks(logf)
    causal = jnp.tril(jnp.ones((L, L), dtype=bool))

    def step(state, inp):
        qt, kt, vt, ft = inp
        bcum = jnp.cumsum(ft, axis=2)
        o_inter = jnp.einsum('bhld,bhdv->bhlv', qt * jnp.exp(bcum), state)
        diff = bcum[:, :, :, None, :] - bcum[:, :, None, :, :]
        decay = jnp.exp(jnp.where(causal[:, :, None], diff, -jnp.inf))
        attn = jnp.einsum('bhtd,bhtsd,bhsd->bhts', qt, decay, kt)
        o = o_inter + jnp.einsum('bhts,bhsv->bhtv', attn, vt)
        blast = bcum[:, :, -1:]
        new_state = (jnp.exp(blast[:, :, 0])[..., None] * state
                     + jnp.einsum('bhsd,bhsv->bhdv', kt * jnp.exp(blast - bcum), vt))
        return new_state, o

    s_fin, o = lax.scan(step, s0.astype(jnp.float32), (qc, kc, vc, fc))
    o = o.transpose(1, 0, 3, 2, 4).reshape(bsz, nc * L, C_HEADS, C_VDIM)[:, :s]
    return o, s_fin

def hybrid_layer(x, kv_buf, conv_buf, h0, s0, lb, norm_g, w_in, conv_w, conv_b,
                 w_a, b_a, w_x, b_x, lam, c_norm_g, w_out):
    bsz, s, _ = x.shape
    h = rmsnorm(x, norm_g)
    z = h @ w_in
    qa, ka, va, ga, xb, gb, qc, fc, ic, gc = split_columns(z)

    qa = qa.reshape(bsz, s, A_HEADS, HEAD_DIM)
    ka = ka.reshape(bsz, s, A_HEADS, HEAD_DIM)
    va = va.reshape(bsz, s, A_HEADS, HEAD_DIM)
    if kv_buf is None:
        branches = [dilated_branch_prompt(qa, ka, va, w, r) for (w, r) in DILATED]
        keep = min(MAX_WINDOW, s)
        k_state, v_state = ka[:, s - keep:], va[:, s - keep:]
    else:
        k_buf, v_buf = kv_buf
        n_buf = k_buf.shape[1]
        k_all = jnp.concatenate([k_buf.astype(ka.dtype), ka], axis=1)
        v_all = jnp.concatenate([v_buf.astype(va.dtype), va], axis=1)
        branches = [dilated_branch_sample(qa, k_all, v_all, w, r, n_buf) for (w, r) in DILATED]
        k_state, v_state = ka, va
    o_a = combine_by_denominator(branches).reshape(bsz, s, A_WIDTH) * jax.nn.silu(ga.astype(jnp.float32))

    x_pad = jnp.concatenate([conv_buf.astype(xb.dtype), xb], axis=1)
    xc = causal_conv(x_pad, conv_w, conv_b)
    hb, h_last = rg_lru(xc, h0, w_a, b_a, w_x, b_x, lam)
    o_b = hb * jax.nn.silu(gb.astype(jnp.float32))
    conv_state = x_pad[:, -(CONV_W - 1):]

    q = jax.nn.silu(qc.astype(jnp.float32)).reshape(bsz, s, C_HEADS, C_KDIM) * (C_KDIM ** -0.5)
    lbh = lb.reshape(C_HEADS, C_KDIM)
    g = lbh + (1.0 - lbh) * jax.nn.sigmoid(fc.astype(jnp.float32)).reshape(bsz, s, C_HEADS, C_KDIM)
    v = ic.astype(jnp.float32).reshape(bsz, s, C_HEADS, C_VDIM)
    oc, s_fin = hgrn2(q, 1.0 - g, v, jnp.log(g), s0)
    oc = oc * lax.rsqrt(jnp.mean(oc * oc, axis=-1, keepdims=True) + RMS_EPS)
    oc = (oc * c_norm_g.astype(jnp.float32).reshape(C_HEADS, C_VDIM)).reshape(bsz, s, C_VWIDTH)
    o_c = oc * jax.nn.silu(gc.astype(jnp.float32))

    mixed = jnp.concatenate([o_a, o_b, o_c], axis=-1).astype(x.dtype)
    y = x + mixed @ w_out
    return y, (k_state, v_state, conv_state, h_last, s_fin)

def setup_inputs(seed: int = 0) -> dict:
    key = jax.random.key(seed)
    ks = jax.random.split(key, 20)
    f32 = jnp.float32
    w_buf = min(MAX_WINDOW, PAST_LEN)
    nrm = lambda k, shape: jax.random.normal(k, shape, dtype=f32)
    return {
        'x_prompt': nrm(ks[0], (BATCH, SEQ, D_MODEL)),
        'x_sample': nrm(ks[1], (DEC_BATCH, DEC_SEQ, D_MODEL)),
        'cache_k_win': nrm(ks[2], (DEPTH, DEC_BATCH, w_buf, A_HEADS, HEAD_DIM)),
        'cache_v_win': nrm(ks[3], (DEPTH, DEC_BATCH, w_buf, A_HEADS, HEAD_DIM)),
        'state_conv': 0.5 * nrm(ks[4], (DEPTH, DEC_BATCH, CONV_W - 1, LRU_WIDTH)),
        'state_lru': 0.5 * nrm(ks[5], (DEPTH, DEC_BATCH, LRU_WIDTH)),
        'state_hgrn': 0.3 * nrm(ks[6], (DEPTH, DEC_BATCH, C_HEADS, C_KDIM, C_VDIM)),
        'norm_g': 1.0 + 0.02 * nrm(ks[7], (DEPTH, D_MODEL)),
        'w_in': nrm(ks[8], (DEPTH, D_MODEL, IN_WIDTH)) * D_MODEL ** -0.5,
        'conv_w': nrm(ks[9], (DEPTH, CONV_W, LRU_WIDTH)) * CONV_W ** -0.5,
        'conv_b': 0.01 * nrm(ks[10], (DEPTH, LRU_WIDTH)),
        'lru_w_a': nrm(ks[11], (DEPTH, LRU_BLOCKS, LRU_BLOCK_DIM, LRU_BLOCK_DIM)) * LRU_BLOCK_DIM ** -0.5,
        'lru_b_a': 0.01 * nrm(ks[12], (DEPTH, LRU_WIDTH)),
        'lru_w_x': nrm(ks[13], (DEPTH, LRU_BLOCKS, LRU_BLOCK_DIM, LRU_BLOCK_DIM)) * LRU_BLOCK_DIM ** -0.5,
        'lru_b_x': 0.01 * nrm(ks[14], (DEPTH, LRU_WIDTH)),
        'lru_lambda': jax.random.uniform(ks[15], (DEPTH, LRU_WIDTH), dtype=f32, minval=4.3, maxval=9.0),
        'hgrn_lb_logits': 0.1 * nrm(ks[16], (DEPTH, C_KWIDTH)),
        'hgrn_norm_g': 1.0 + 0.02 * nrm(ks[17], (DEPTH, C_VWIDTH)),
        'w_out': nrm(ks[18], (DEPTH, MIX_WIDTH, D_MODEL)) * MIX_WIDTH ** -0.5,
        'final_norm_g': 1.0 + 0.02 * nrm(ks[19], (D_MODEL,)),
    }

def reference(x_prompt, x_sample, cache_k_win, cache_v_win, state_conv, state_lru, state_hgrn,
              norm_g, w_in, conv_w, conv_b, lru_w_a, lru_b_a, lru_w_x, lru_b_x, lru_lambda,
              hgrn_lb_logits, hgrn_norm_g, w_out, final_norm_g):
    lb_w = jax.nn.softmax(hgrn_lb_logits.astype(jnp.float32), axis=0)
    lb_all = jnp.cumsum(lb_w, axis=0) - lb_w[0]
    bp = x_prompt.shape[0]
    xp, xs = x_prompt, x_sample
    sp, ss = [], []
    for l in range(DEPTH):
        lw = (norm_g[l], w_in[l], conv_w[l], conv_b[l], lru_w_a[l], lru_b_a[l], lru_w_x[l], lru_b_x[l],
              lru_lambda[l], hgrn_norm_g[l], w_out[l])
        xp, st_p = hybrid_layer(
            xp, None,
            jnp.zeros((bp, CONV_W - 1, LRU_WIDTH), dtype=xp.dtype),
            jnp.zeros((bp, LRU_WIDTH), dtype=jnp.float32),
            jnp.zeros((bp, C_HEADS, C_KDIM, C_VDIM), dtype=jnp.float32),
            lb_all[l], *lw)
        xs, st_s = hybrid_layer(
            xs, (cache_k_win[l], cache_v_win[l]), state_conv[l], state_lru[l], state_hgrn[l],
            lb_all[l], *lw)
        sp.append(st_p)
        ss.append(st_s)
    y_prompt = rmsnorm(xp, final_norm_g)
    y_sample = rmsnorm(xs, final_norm_g)
    k_win_prompt = jnp.stack([t[0] for t in sp])
    v_win_prompt = jnp.stack([t[1] for t in sp])
    k_win_sample = jnp.stack([t[0] for t in ss])
    v_win_sample = jnp.stack([t[1] for t in ss])
    conv_prompt = jnp.stack([t[2] for t in sp])
    conv_sample = jnp.stack([t[2] for t in ss])
    lru_prompt = jnp.stack([t[3] for t in sp])
    lru_sample = jnp.stack([t[3] for t in ss])
    hgrn_prompt = jnp.stack([t[4] for t in sp])
    hgrn_sample = jnp.stack([t[4] for t in ss])
    return (y_prompt, y_sample, k_win_prompt, v_win_prompt, k_win_sample, v_win_sample,
            conv_prompt, conv_sample, lru_prompt, lru_sample, hgrn_prompt, hgrn_sample)


_drawn_inputs = setup_inputs


def setup_inputs(seed=0):
    import zlib

    import numpy as np

    out = dict(_drawn_inputs(seed))
    spreads = {}
    factors = {'state_hgrn': 4.867,
     'lru_b_a': 21.791,
     'lru_b_x': 23.594,
     'hgrn_norm_g': 25.771,
     'final_norm_g': 8.0,
     'cache_k_win': 6.073,
     'cache_v_win': 4.733}
    for name, (base, spread) in spreads.items():
        noise = np.random.default_rng([zlib.crc32(name.encode()), seed]).standard_normal(out[name].shape)
        drawn = base * np.exp(spread * noise) if base else spread * noise
        out[name] = jnp.asarray(drawn.astype(out[name].dtype))
    for name, factor in factors.items():
        out[name] = (out[name] * factor).astype(out[name].dtype)
    return out
```

```python
from contextlib import ExitStack, contextmanager

import numpy as np

import concourse.bass as bass
from concourse import mybir

F32 = mybir.dt.float32
F32R = mybir.dt.float32r
I32 = mybir.dt.int32
ALU = mybir.AluOpType
ACT = mybir.ActivationFunctionType
AX_X = mybir.AxisListType.X

P = 128
D = 1024
KD = D // P
SEQ = 2048
NB, NT = 8, 8
NS = NB * NT
T = SEQ + NS
NTILE = SEQ // P
EPS = 1e-6
HD = 64
NH = 6
AW = NH * HD
WIN = 2048
IN_W = 4608
GROUPS = [(g * 512, 512) for g in range(SEQ // 512)] + [(SEQ, NS)]
NF = 24
ZQ, ZK, ZXB, ZGB, ZQC, ZFC = 0, 3, 6, 9, 12, 18
TW = 192
NTG = 10
TK, TV, TGA, TIC, TGC = 0, 384, 768, 1152, 1536
TCOLS = NTG * TW
NEG = -1.0e30
BASE = 1
DILATED = ((128, 1), (512, 4), (2048, 16))
SCALE = HD ** -0.5


def mm3(nc, out, w_hi, w_lo, m_hi, m_lo, start, stop):
    nc.tensor.matmul(out, w_hi, m_hi, start=start, stop=False)
    nc.tensor.matmul(out, w_hi, m_lo, start=False, stop=False)
    return nc.tensor.matmul(out, w_lo, m_hi, start=False, stop=stop)


def hold(eng, sem):
    eng.sem_inc(sem, 1)


class Chain:

    def __init__(self, eng, sem, base=0):
        self.eng, self.sem, self.n, self.base = eng, sem, 0, base

    def mark(self, ins):
        self.n += 1
        ins.then_inc(self.sem, 1)
        return self.base + self.n

    def link(self, ins):
        self.eng.wait_ge(self.sem, BASE + self.mark(ins))


def constants(nc, sem, con):
    made = sem("c_made")
    with nc.Block() as block:
        @block.gpsimd
        def _(pool):
            nc.gpsimd.memset(con["one"][:], 1.0).then_inc(made, 1)
            nc.gpsimd.memset(con["mhalf"][:], -0.5).then_inc(made, 1)
            pool.wait_ge(made, BASE + 2)
            nc.gpsimd.affine_select(out=con["ident"][:], in_=con["one"][:], pattern=[[-1, P]], compare_op=ALU.is_equal,
                                    fill=0.0, base=0, channel_multiplier=1).then_inc(made, 1)
            pool.wait_ge(made, BASE + 3)


def norm_and_turn(nc, sem, g, io, con, ht):
    with ExitStack() as ctx:
        def sb(name, shape, dt=F32):
            return ctx.enter_context(nc.sbuf_tensor(name, shape, dt))

        xt = [sb(f"n_x{p}", [P, D]) for p in range(3)]
        xn = [sb(f"n_xn{p}", [P, D]) for p in range(2)]
        hf = [sb(f"n_hf{p}", [P, 4, P]) for p in range(2)]
        st = [sb(f"n_st{p}", [P, 4]) for p in range(2)]
        gk = sb("n_gk", [P, KD])
        gfull = sb("n_gfull", [P, KD, P])
        ps = [ctx.enter_context(nc.psum_tensor(f"n_ps{b}", [P, 4, P], F32)) for b in range(4)]

        x_in = [sem(f"n_x_in{p}") for p in range(3)]
        g_in = sem("n_g_in")
        squares = sem("n_squares")
        meansq = sem("n_meansq")
        rstd = sem("n_rstd")
        normed = sem("n_normed")
        turned = sem("n_turned")
        h_full = sem("n_h_full")
        h_hi = sem("n_h_hi")
        h_lo = sem("n_h_lo")
        own = sem("n_own")

        tiles = [(i, i % 2, i * P, P) for i in range(NTILE)] + [(NTILE, 0, SEQ, NS)]
        block = ctx.enter_context(nc.Block())

        @block.sync
        def _(sp):
            sp.dma_start(gk[:], io["norm_g"].rearrange("a (k p) -> p (a k)", p=P), allow_slow_non_contiguous=True).then_inc(g_in, 16)
            for i, p, t0, n in tiles:
                if i >= 3:
                    sp.wait_ge(normed, BASE + i - 2)
                src = io["xp"][t0:t0 + n, :] if t0 < SEQ else io["xs"]
                sp.dma_start(xt[i % 3][:n, :], src).then_inc(x_in[i % 3], 16)

        @block.gpsimd
        def _(pool):
            for i, p, t0, n in tiles:
                pool.wait_ge(meansq, BASE + i + 1)
                nc.gpsimd.tensor_tensor(st[p][:n, 2:3], st[p][:n, 1:2], con["mhalf"][:n, 0:1], ALU.pow).then_inc(rstd, 1)

        @block.scalar
        def _(act):
            def square(i, p, t0, n):
                act.wait_ge(x_in[i % 3], BASE + 16 * (i // 3 + 1))
                if i >= 2:
                    act.wait_ge(turned, BASE + 2 * (i - 1))
                nc.scalar.activation(xn[p][:n, :], xt[i % 3][:n, :], ACT.Square, accum_out=st[p][:n, 0:1]).then_inc(squares, 1)

            def high(i, p, t0, n):
                for q in range(2):
                    act.wait_ge(h_full, BASE + 2 * i + q + 1)
                    dst = ht[0][:, 4 * q:4 * q + 4, t0:t0 + n]
                    nc.scalar.activation(dst, hf[q][:, :, :n], ACT.Copy).then_inc(h_hi, 1)

            for i in range(len(tiles) + 1):
                if i < len(tiles):
                    square(*tiles[i])
                if i >= 1:
                    high(*tiles[i - 1])

        @block.vector
        def _(dve):
            own_steps = Chain(dve, own)
            dve.wait_ge(g_in, BASE + 16)
            for k in range(KD):
                own_steps.mark(nc.vector.tensor_scalar(gfull[:, k, :], con["one"][:], gk[:, k:k + 1], None, ALU.mult))
            dve.wait_ge(own, BASE + KD)

            def norm(i, p, t0, n):
                dve.wait_ge(squares, BASE + i + 1)
                nc.vector.tensor_scalar(st[p][:n, 1:2], st[p][:n, 0:1], 1.0 / D, EPS, ALU.mult, ALU.add).then_inc(meansq, 1)
                dve.wait_ge(rstd, BASE + i + 1)
                nc.vector.tensor_scalar(xn[p][:n, :], xt[i % 3][:n, :], st[p][:n, 2:3], None, ALU.mult).then_inc(normed, 1)

            def split(i, p, t0, n):
                for q in range(2):
                    j = 2 * i + q
                    dve.wait_ge(turned, BASE + j + 1)
                    if j >= 2:
                        dve.wait_ge(h_hi, BASE + j - 1)
                        dve.wait_ge(h_lo, BASE + j - 1)
                    nc.vector.tensor_tensor(hf[q][:, :, :n], ps[j % 4][:, :, :n], gfull[:, 4 * q:4 * q + 4, :n],
                                            ALU.mult).then_inc(h_full, 1)
                for q in range(2):
                    j = 2 * i + q
                    dve.wait_ge(h_hi, BASE + j + 1)
                    nc.vector.tensor_tensor(ht[1][:, 4 * q:4 * q + 4, t0:t0 + n], hf[q][:, :, :n],
                                            ht[0][:, 4 * q:4 * q + 4, t0:t0 + n], ALU.subtract).then_inc(h_lo, 1)

            for i in range(len(tiles) + 1):
                if i < len(tiles):
                    norm(*tiles[i])
                if i >= 1:
                    split(*tiles[i - 1])

        @block.tensor
        def _(pe):
            for i, p, t0, n in tiles:
                pe.wait_ge(normed, BASE + i + 1)
                for q in range(2):
                    j = 2 * i + q
                    if j >= 4:
                        pe.wait_ge(h_full, BASE + j - 3)
                    for k in range(4):
                        c = (4 * q + k) * P
                        mm = nc.tensor.transpose(ps[j % 4][:, k, :n], xn[p][:n, c:c + P], con["ident"][:n, :n])
                    mm.then_inc(turned, 1)


def project(nc, sem, io, ht, zf, zt):
    w_v = io["w_in"].rearrange("(k p) c -> p k c", p=P)
    with ExitStack() as ctx:
        def sb(name, shape, dt=F32):
            return ctx.enter_context(nc.sbuf_tensor(name, shape, dt))

        w_raw = [sb(f"p_wraw{p}", [P, KD * TW]) for p in range(2)]
        w_hi = [sb(f"p_whi{p}", [P, KD * TW], F32R) for p in range(2)]
        w_lo = [sb(f"p_wlo{p}", [P, KD * TW], F32R) for p in range(2)]
        stage = [sb(f"p_stage{p}", [P, T]) for p in range(2)]
        RING = 8
        ring = [stage[r // 4][:, (r % 4) * TW:(r % 4 + 1) * TW] for r in range(RING)]
        bank = [ctx.enter_context(nc.psum_tensor(f"p_bank{b}", [P, 512], F32)) for b in range(8)]

        w_in_f = [sem(f"pf_w_in{p}") for p in range(2)]
        w_split = sem("pf_w_split")
        w_high = sem("pf_w_high")
        w_used = sem("pf_w_used")
        z_sum = sem("pf_z_sum")
        z_out = sem("pf_z_out")
        z_store = [sem(f"pf_z_store{p}") for p in range(2)]

        def views(n):
            v = lambda t: t[:, 0:KD * n].rearrange("p (k c) -> p k c", c=n)
            return [v(t) for t in w_raw], [v(t) for t in w_hi], [v(t) for t in w_lo]

        raw, hi, lo = views(P)
        SPANS = [(0, 3, 0), (3, 12, 6)]

        G = len(GROUPS)
        with nc.Block() as block:
            @block.sync
            def _(sp):
                for a, b, skip in SPANS:
                    with sp.Fori(a, b) as i:
                        for p in range(2):
                            sp.wait_ge(w_split, BASE + 2 * i + p + 1)
                            sp.dma_start(raw[p], w_v[:, :, bass.ds((2 * i + p + skip) * P, P)]).then_inc(w_in_f[p], 16)

            @block.scalar
            def _(act):
                act.sem_inc(z_out, G)
                with act.Fori(0, NF // 2) as i:
                    for p in range(2):
                        act.wait_ge(z_store[p], BASE + 16 * i)
                        for g, (t0, n) in enumerate(GROUPS):
                            act.wait_ge(z_sum, BASE + G * (2 * i + p + 1) + g + 1)
                            nc.scalar.activation(stage[p][:, t0:t0 + n], bank[g][:, :n], ACT.Copy).then_inc(z_out, 1)
                        act.wait_ge(z_out, BASE + G * (2 * i + p + 2))
                        act.dma_start(zf[bass.ds((2 * i + p) * P, P), :], stage[p][:, 0:T]).then_inc(z_store[p], 16)
                for p in range(2):
                    act.wait_ge(z_store[p], BASE + 16 * NF // 2)

            @block.vector
            def _(dve):
                dve.sem_inc(w_split, 2)
                with dve.Fori(0, NF // 2) as i:
                    for p in range(2):
                        dve.wait_ge(w_in_f[p], BASE + 16 * i + 16)
                        dve.wait_ge(z_sum, BASE + G * (2 * i + p))
                        nc.vector.tensor_copy(hi[p], raw[p]).then_inc(w_high, 1)
                        dve.wait_ge(w_high, BASE + 2 * i + p + 1)
                        nc.vector.tensor_tensor(lo[p], raw[p], hi[p], ALU.subtract).then_inc(w_split, 1)

            @block.tensor
            def _(pe):
                pe.sem_inc(z_sum, G)
                with pe.Fori(0, NF // 2) as i:
                    for p in range(2):
                        pe.wait_ge(w_split, BASE + 2 * i + p + 3)
                        for g, (t0, n) in enumerate(GROUPS):
                            pe.wait_ge(z_out, BASE + G * (2 * i + p) + g + 1)
                            for k in range(KD):
                                mm = mm3(nc, bank[g][:, :n], hi[p][:, k, :], lo[p][:, k, :],
                                         ht[0][:, k, t0:t0 + n], ht[1][:, k, t0:t0 + n], k == 0, k == KD - 1)
                            mm.then_inc(z_sum, 1)

        raw, hi, lo = views(TW)
        TILES = [(j * P, P) for j in range(NTILE)] + [(SEQ, NS)]
        N = len(TILES)
        w_in_t = [sem(f"pt_w_in{p}") for p in range(2)]
        t_high = sem("pt_w_high")
        t_split = sem("pt_w_split")
        t_sum = sem("pt_z_sum")
        t_out = sem("pt_z_out")
        t_store = [sem(f"pt_z_store{r}") for r in range(RING)]
        uses = [len(range(r, N, RING)) for r in range(RING)]
        SPANS = [(0, 3, AW), (3, 5, IN_W - 4 * TW - 6 * TW)]
        with nc.Block() as block:
            @block.sync
            def _(sp):
                for a, b, skip in SPANS:
                    with sp.Fori(a, b) as i:
                        for p in range(2):
                            sp.wait_ge(t_split, BASE + 2 * i + p + 1)
                            sp.dma_start(raw[p], w_v[:, :, bass.ds((2 * i + p) * TW + skip, TW)]).then_inc(w_in_t[p], 16)

            @block.scalar
            def _(act):
                act.sem_inc(t_out, N)
                with act.Fori(0, NTG) as i:
                    for j, (t0, n) in enumerate(TILES):
                        act.wait_ge(t_sum, BASE + N * i + N + j + 1)
                        act.wait_ge(t_store[j % RING], BASE + 16 * uses[j % RING] * i + 16 * (j // RING))
                        nc.scalar.activation(ring[j % RING][:n, :], bank[j % 8][:n, :TW], ACT.Copy).then_inc(t_out, 1)
                        act.wait_ge(t_out, BASE + N * i + N + j + 1)
                        act.dma_start(zt[t0:t0 + n, bass.ds(i * TW, TW)], ring[j % RING][:n, :]).then_inc(t_store[j % RING], 16)
                for r in range(RING):
                    act.wait_ge(t_store[r], BASE + 16 * NTG * uses[r])

            @block.vector
            def _(dve):
                dve.sem_inc(t_split, 2)
                with dve.Fori(0, NTG // 2) as i:
                    for p in range(2):
                        dve.wait_ge(w_in_t[p], BASE + 16 * i + 16)
                        dve.wait_ge(t_sum, BASE + N * (2 * i + p))
                        nc.vector.tensor_copy(hi[p], raw[p]).then_inc(t_high, 1)
                        dve.wait_ge(t_high, BASE + 2 * i + p + 1)
                        nc.vector.tensor_tensor(lo[p], raw[p], hi[p], ALU.subtract).then_inc(t_split, 1)

            @block.tensor
            def _(pe):
                pe.sem_inc(t_sum, N)
                with pe.Fori(0, NTG // 2) as i:
                    for p in range(2):
                        pe.wait_ge(t_split, BASE + 2 * i + p + 3)
                        for j, (t0, n) in enumerate(TILES):
                            last = N + j - 8 if j >= 8 else (8 * ((N - 1 - j) // 8) + j)
                            pe.wait_ge(t_out, BASE + N * (2 * i + p) + last + 1)
                            for k in range(KD):
                                mm = mm3(nc, bank[j % 8][:n, :TW], ht[0][:, k, t0:t0 + n], ht[1][:, k, t0:t0 + n],
                                         hi[p][:, k, :], lo[p][:, k, :], k == 0, k == KD - 1)
                            mm.then_inc(t_sum, 1)


def lru(nc, sem, io, con, zf, mb):
    NC3 = AW // P
    XPAD = 3 + SEQ
    with ExitStack() as ctx:
        def sb(name, shape, dt=F32):
            return ctx.enter_context(nc.sbuf_tensor("l_" + name, shape, dt))

        xpad = [sb(f"xpad{p}", [P, XPAD + NB * 11]) for p in range(2)]
        gb = [sb(f"gb{p}", [P, T]) for p in range(2)]
        xc, rg, ig, sg, sq, hh = (sb(n, [P, T]) for n in ("xc", "rg", "ig", "sg", "sq", "hh"))
        ob = [sb(f"ob{p}", [P, T]) for p in range(2)]
        wbd = sb("wbd", [P, 2, NC3, P])
        cw = sb("cw", [P, NC3, 4])
        cst = sb("cst", [P, NC3, NB * 3])
        cso = sb("cso", [P, NC3, NB * 3])
        h0 = sb("h0", [P, NC3, NB])
        vec = sb("vec", [P, 4, NC3])
        par = sb("par", [P, 8, NC3])
        ps = [ctx.enter_context(nc.psum_tensor(f"l_ps{b}", [P, 512], F32)) for b in range(8)]
        x_in = [sem(f"l_x_in{c}") for c in range(NC3)]
        par_in = sem("l_par_in")
        zeroed = sem("l_zeroed")
        par_act = sem("l_par_act")
        dve_own = sem("l_dve_own")
        params = sem("l_params")
        conv = sem("l_conv")
        gate_sum = sem("l_gate_sum")
        gates = sem("l_gates")
        decay = sem("l_decay")
        root = sem("l_root")
        g_sig = sem("l_g_sig")
        g_silu = sem("l_g_silu")
        scanned = sem("l_scanned")
        mixed = sem("l_mixed")
        store = sem("l_store")
        smp = [xpad[p][:, XPAD:].rearrange("p (b j) -> p b j", j=11) for p in range(2)]
        per_b = lambda t, o=0: t[:, SEQ:T].rearrange("p (b t) -> p b t", t=NT)
        block = ctx.enter_context(nc.Block())

        @block.sync
        def _(sp):
            kw = dict(allow_slow_non_contiguous=True)
            sp.wait_ge(zeroed, BASE + 1)
            for g, name in enumerate(("lru_w_a", "lru_w_x")):
                for hp in range(2):
                    w = io[name].rearrange("a (c h) i j -> i (a c) h j", h=2)
                    sp.dma_start(wbd[hp * HD:(hp + 1) * HD, g, :, hp * HD:(hp + 1) * HD], w[:, :, hp, :]).then_inc(par_in, 16)
            for c in range(NC3):
                sp.dma_start(cw[:, c, :], io["conv_w"].rearrange("a j (c p) -> p (a c) j", p=P)[:, c, :], **kw).then_inc(par_in, 16)
                sp.dma_start(cst[:, c, :], io["state_conv"].rearrange("a b j (c p) -> p (a c) (b j)", p=P)[:, c, :], **kw).then_inc(par_in, 16)
                sp.dma_start(h0[:, c, :], io["state_lru"].rearrange("a b (c p) -> p (a c) b", p=P)[:, c, :], **kw).then_inc(par_in, 16)
            for n, name in enumerate(("conv_b", "lru_b_a", "lru_b_x", "lru_lambda")):
                sp.dma_start(vec[:, n, :], io[name].rearrange("a (c p) -> p (a c)", p=P), **kw).then_inc(par_in, 16)
            def load(c):
                p = c % 2
                rows = zf[(ZXB + c) * P:(ZXB + c + 1) * P, :]
                sp.dma_start(xpad[p][:, 3:XPAD], rows[:, 0:SEQ]).then_inc(x_in[c], 16)
                sp.dma_start(smp[p][:, :, 3:11], rows[:, SEQ:T].rearrange("p (b t) -> p b t", t=NT)).then_inc(x_in[c], 16)
                sp.dma_start(gb[p][:, :], zf[(ZGB + c) * P:(ZGB + c + 1) * P, :]).then_inc(x_in[c], 16)

            def save(c):
                p = c % 2
                cs = slice(c * P, (c + 1) * P)
                sp.wait_ge(scanned, BASE + c + 1)
                sp.dma_start(io["conv_prompt"].rearrange("a j c -> c a j")[cs, 0, :], xpad[p][:, SEQ:XPAD], **kw).then_inc(store, 16)
                sp.dma_start(io["conv_sample"].rearrange("b j c -> c (b j)")[cs, :], cso[:, c, :], **kw).then_inc(store, 16)
                sp.dma_start(io["lru_prompt"].rearrange("a c -> c a")[cs, :], hh[:, SEQ - 1:SEQ], **kw).then_inc(store, 16)
                sp.dma_start(io["lru_sample"].rearrange("b c -> c b")[cs, :], per_b(hh)[:, :, NT - 1], **kw).then_inc(store, 16)
                sp.wait_ge(mixed, BASE + c + 1)
                sp.dma_start(mb[cs, :], ob[p][:]).then_inc(store, 16)
                sp.wait_ge(store, BASE + 16 * 5 * (c + 1))

            for c in range(NC3 + 2):
                if c >= 2:
                    save(c - 2)
                if c < NC3:
                    load(c)

        @block.gpsimd
        def _(pool):
            nc.gpsimd.memset(wbd[:], 0.0).then_inc(zeroed, 1)
            kw = dict(allow_slow_non_contiguous=True)
            for c in range(NC3):
                p = c % 2
                pool.wait_ge(g_sig, BASE + c + 1)
                if c >= 2:
                    pool.wait_ge(store, BASE + 16 * 5 * (c - 1))
                nc.gpsimd.tensor_tensor(ob[p][:], gb[p][:], sg[:], ALU.mult).then_inc(g_silu, 1)
                pool.wait_ge(g_silu, BASE + c + 1)
                pool.wait_ge(scanned, BASE + c + 1)
                nc.gpsimd.tensor_tensor(ob[p][:], ob[p][:], hh[:], ALU.mult).then_inc(mixed, 1)

        @block.scalar
        def _(act):
            act.wait_ge(par_act, BASE + 1)
            nc.scalar.activation(par[:, 1, :], par[:, 0, :], ACT.Exp).then_inc(par_act, 1)
            for c in range(NC3):
                if c:
                    act.wait_ge(scanned, BASE + c)
                    act.wait_ge(mixed, BASE + c)
                act.wait_ge(x_in[c], BASE + 48)
                nc.scalar.activation(sg[:], gb[c % 2][:], ACT.Sigmoid).then_inc(g_sig, 1)
                for g, (t0, n) in enumerate(GROUPS):
                    for k, dst in enumerate((rg, ig)):
                        m = 2 * len(GROUPS) * c + 2 * g + k
                        act.wait_ge(gate_sum, BASE + m + 1)
                        nc.scalar.activation(dst[:, t0:t0 + n], ps[m % 8][:, :n], ACT.Sigmoid,
                                             bias=vec[:, 1 + k, c:c + 1]).then_inc(gates, 1)
                act.wait_ge(gates, BASE + 2 * len(GROUPS) * (c + 1))
                act.wait_ge(params, BASE + 1)
                nc.scalar.activation(sq[:], rg[:], ACT.Tanh, scale=par[:, 7, c:c + 1]).then_inc(root, 1)
                act.wait_ge(root, BASE + 2 * c + 1)
                nc.scalar.activation(rg[:], rg[:], ACT.Exp, scale=par[:, 6, c:c + 1]).then_inc(decay, 1)
                nc.scalar.activation(sq[:], sq[:], ACT.Sqrt).then_inc(root, 1)

        @block.vector
        def _(dve):
            own = Chain(dve, dve_own)
            V = nc.vector
            dve.wait_ge(par_in, BASE + 16 * (4 + 3 * NC3 + 4))
            lam = vec[:, 3, :]
            own.link(V.tensor_scalar(par[:, 2, :], lam, -1.0, None, ALU.mult))
            V.tensor_tensor(par[:, 0, :], par[:, 2, :], lam, ALU.min).then_inc(par_act, 1)
            dve.wait_ge(par_act, BASE + 2)
            own.link(V.tensor_scalar(par[:, 3, :], par[:, 1, :], 2.0, None, ALU.add))
            own.link(V.reciprocal(par[:, 3, :], par[:, 3, :]))
            own.link(V.tensor_tensor(par[:, 3, :], par[:, 3, :], par[:, 1, :], ALU.mult))
            own.link(V.tensor_tensor(par[:, 4, :], par[:, 3, :], par[:, 3, :], ALU.mult))
            own.link(V.tensor_scalar(par[:, 5, :], par[:, 4, :], 1.0 / 17, None, ALU.mult))
            for odd in range(15, 2, -2):
                own.link(V.scalar_tensor_tensor(out=par[:, 5, :], in0=par[:, 5, :], scalar=1.0 / odd, in1=par[:, 4, :],
                                                op0=ALU.add, op1=ALU.mult))
            own.link(V.scalar_tensor_tensor(out=par[:, 5, :], in0=par[:, 5, :], scalar=1.0, in1=par[:, 3, :],
                                            op0=ALU.add, op1=ALU.mult))
            own.link(V.tensor_scalar(par[:, 2, :], par[:, 2, :], 0.0, None, ALU.max))
            own.link(V.scalar_tensor_tensor(out=par[:, 2, :], in0=par[:, 5, :], scalar=2.0, in1=par[:, 2, :],
                                            op0=ALU.mult, op1=ALU.add))
            own.link(V.tensor_scalar(par[:, 6, :], par[:, 2, :], -8.0, None, ALU.mult))
            V.tensor_scalar(par[:, 7, :], par[:, 6, :], -0.5, None, ALU.mult).then_inc(params, 1)
            for c in range(NC3):
                p = c % 2
                dve.wait_ge(x_in[c], BASE + 48)
                if c:
                    dve.wait_ge(gate_sum, BASE + 2 * len(GROUPS) * c)
                own.mark(V.memset(xpad[p][:, 0:3], 0.0))
                own.link(V.tensor_copy(smp[p][:, :, 0:3], cst[:, c, :].rearrange("p (b j) -> p b j", j=3)))
                parts = [(xc[:, 0:SEQ], lambda j: xpad[p][:, j:j + SEQ]), (per_b(xc), lambda j: smp[p][:, :, j:j + NT])]
                for j in range(4):
                    for n, (dst, src) in enumerate(parts):
                        if j == 0:
                            ins = V.tensor_scalar(dst, src(0), cw[:, c, 0:1], vec[:, 0, c:c + 1], ALU.mult, ALU.add)
                        else:
                            ins = V.scalar_tensor_tensor(out=dst, in0=src(j), scalar=cw[:, c, j:j + 1], in1=dst,
                                                         op0=ALU.mult, op1=ALU.add)
                        (own.mark if n == 0 else own.link)(ins)
                V.tensor_copy(cso[:, c, :].rearrange("p (b j) -> p b j", j=3), smp[p][:, :, 8:11]).then_inc(conv, 1)
                dve.wait_ge(gates, BASE + 2 * len(GROUPS) * (c + 1))
                own.link(V.tensor_tensor(ig[:], ig[:], xc[:], ALU.mult))
                dve.wait_ge(decay, BASE + c + 1)
                dve.wait_ge(root, BASE + 2 * c + 2)
                own.link(V.scalar_tensor_tensor(out=sq[:], in0=rg[:], scalar=1.0, in1=sq[:], op0=ALU.add, op1=ALU.mult))
                own.link(V.tensor_tensor(ig[:], ig[:], sq[:], ALU.mult))
                own.link(V.tensor_tensor(h0[:, c, :], h0[:, c, :], per_b(rg)[:, :, 0], ALU.mult))
                own.link(V.tensor_tensor(per_b(ig)[:, :, 0], per_b(ig)[:, :, 0], h0[:, c, :], ALU.add))
                own.link(V.memset(per_b(rg)[:, :, 0], 0.0))
                if c:
                    dve.wait_ge(mixed, BASE + c)
                    dve.wait_ge(store, BASE + 16 * 5 * c)
                V.tensor_tensor_scan(hh[:], rg[:], ig[:], 0.0, ALU.mult, ALU.add).then_inc(scanned, 1)

        @block.tensor
        def _(pe):
            pe.wait_ge(par_in, BASE + 16 * (4 + 3 * NC3 + 4))
            for c in range(NC3):
                pe.wait_ge(conv, BASE + c + 1)
                for g, (t0, n) in enumerate(GROUPS):
                    for k in range(2):
                        m = 2 * len(GROUPS) * c + 2 * g + k
                        if m >= 8:
                            pe.wait_ge(gates, BASE + m - 7)
                        nc.tensor.matmul(ps[m % 8][:, :n], wbd[:, k, c, :], xc[:, t0:t0 + n], start=True,
                                         stop=True).then_inc(gate_sum, 1)


def hgrn(nc, sem, io, con, zf, zt, mt):
    W = NH * P
    HALVES = [64, 32, 16, 8, 4, 2, 1]
    NL = len(HALVES)
    NM = NL + 1
    with ExitStack() as ctx:
        def sb(name, shape, dt=F32):
            return ctx.enter_context(nc.sbuf_tensor("h_" + name, shape, dt))

        two = lambda name, shape: [sb(f"{name}{p}", shape) for p in range(2)]
        qc, fc, vv, gc = two("qc", [P, W]), two("fc", [P, W]), two("vv", [P, AW]), two("gc", [P, AW])
        sq, gg, kk, bb = two("sq", [P, W]), two("gg", [P, W]), two("kk", [P, W]), two("bb", [P, W])
        qd, kd, kdt = two("qd", [P, W]), two("kd", [P, W]), two("kdt", [P, W])
        sg, oc = two("sg", [P, AW]), two("oc", [P, AW])
        attn = two("attn", [P, NH, P])
        attn_s = sb("attn_s", [P, NH, P])
        glast, small = two("glast", [P, NH]), two("small", [P, 4, NH])
        lev = [sb(f"lev{l}", [P, W]) for l in range(NL)]
        mask = [sb(f"mask{l}", [P, P]) for l in range(NL)]
        one, omf = sb("one", [P, W]), sb("omf", [P, W])
        qr, gsig, lg = two("qr", [P, W]), two("gsig", [P, AW]), sb("lg", [P, W])
        cut, cut_s = sb("cut", [P, W]), sb("cut_s", [P, NH * NS])
        gnf = sb("gnf", [P, AW])
        lbl = sb("lbl", [P, 4, NH])
        state, stmp, sqo = sb("state", [P, AW]), sb("stmp", [P, AW]), sb("sqo", [P, AW])
        s0 = sb("s0", [P, NB, AW])
        qdb = sb("qdb", [P, NB, NH * NS])
        vb = sb("vb", [NS, NB, AW])
        rowm = sb("rowm", [NS, NB])
        lp = [ctx.enter_context(nc.psum_tensor(f"h_lp{b}", [P, 1024], F32)) for b in range(2)]
        tp = ctx.enter_context(nc.psum_tensor("h_tp", [P, 1024], F32))
        op = ctx.enter_context(nc.psum_tensor("h_op", [P, 512], F32))
        up = ctx.enter_context(nc.psum_tensor("h_up", [P, 512], F32))

        ld_fg = [sem(f"h_ld_fg{p}") for p in range(2)]
        ld_q = [sem(f"h_ld_q{p}") for p in range(2)]
        ld_v = [sem(f"h_ld_v{p}") for p in range(2)]
        names = ("par_in", "const", "setup", "sig", "gated", "g_ready", "log_g", "q_ready", "k_ready", "b_ready",
                 "exp_b", "dif_l", "exp_l", "qd_ready", "kd_ready", "g_last", "diff", "expd", "xlev", "pairs", "taken",
                 "kd_turned", "kd_copied", "o_sum", "u_sum", "s_tmp", "s_new", "squared", "stat", "scaled", "out",
                 "gate_a", "gate_b", "normed", "qdb_r", "vb_r", "us", "fin", "held")
        S = {n: sem("h_" + n) for n in names}
        s_gl = sb("s_gl", [P, NB * NH])
        ub = [up, tp]
        ost = [sem(f"h_ost{p}") for p in range(2)]

        def heads(t, n):
            return t[:, 0:NH * n].rearrange("p (h t) -> p h t", h=NH)

        def blocks(t, n, hs):
            return t[:, 0:NH * n].rearrange("p (c w) -> p c w", w=2 * hs)

        def levels(n):
            return [l for l in range(NL) if 2 * HALVES[l] <= (P if n == P else NT)]

        with nc.Block() as block:
            @block.sync
            def _(sp):
                sp.dma_start(lbl[:, 0, :], io["hgrn_lb_logits"].rearrange("a (h p) -> p (a h)", p=P),
                             allow_slow_non_contiguous=True).then_inc(S["par_in"], 16)
                sp.dma_start(gnf[:], io["hgrn_norm_g"].partition_broadcast(P).rearrange("p a c -> p (a c)")).then_inc(S["par_in"], 16)
                sp.dma_start(s0[:].rearrange("p b (h v) -> p (b h) v", v=HD),
                             io["state_hgrn"].rearrange("b h d v -> d (b h) v")).then_inc(S["par_in"], 16)

            @block.gpsimd
            def _(pool):
                G = nc.gpsimd
                ch = Chain(pool, S["const"])
                for t, v in ((one, 1.0), (cut, 1.0), (cut_s, 1.0), (state, 0.0), (qdb, 0.0), (attn[0], 0.0), (attn[1], 0.0), (attn_s, 0.0)):
                    ch.mark(G.memset(t[:], v))
                for l, hs in enumerate(HALVES):
                    ch.mark(G.memset(mask[l][:], 0.0))
                pool.wait_ge(S["const"], BASE + ch.n)
                ch.mark(G.memset(heads(cut, P)[:, :, 0:1], 0.0))
                ch.mark(G.memset(cut_s[:].rearrange("p (c w) -> p c w", w=NT)[:, :, 0:1], 0.0))
                ch.mark(G.affine_select(out=rowm[:], in_=one[:NS, 0:NB], pattern=[[-NT, NB]], compare_op=ALU.is_ge,
                                        fill=0.0, base=0, channel_multiplier=1))
                for l, hs in enumerate(HALVES):
                    v = mask[l][:].rearrange("p (c w) -> p c w", w=2 * hs)[:, :, hs:]
                    src = one[:, 0:64].rearrange("p (c w) -> p c w", w=hs)
                    ch.mark(G.affine_select(out=v, in_=src, pattern=[[-2 * hs, 64 // hs], [0, hs]], compare_op=ALU.is_ge,
                                            fill=0.0, base=0, channel_multiplier=1))
                pool.wait_ge(S["const"], BASE + ch.n)
                ch.mark(G.affine_select(out=rowm[:], in_=rowm[:], pattern=[[NT, NB]], compare_op=ALU.is_ge,
                                        fill=0.0, base=NT - 1, channel_multiplier=-1))
                for l, hs in enumerate(HALVES):
                    v = mask[l][:].rearrange("p (c w) -> p c w", w=2 * hs)[:, :, hs:]
                    ch.mark(G.affine_select(out=v, in_=v, pattern=[[2 * hs, 64 // hs], [0, hs]], compare_op=ALU.is_ge,
                                            fill=0.0, base=hs - 1, channel_multiplier=-1))
                pool.wait_ge(S["const"], BASE + ch.n)

            @block.scalar
            def _(act):
                act.wait_ge(S["setup"], BASE + 1)
                nc.scalar.activation(lbl[:, 2, :], lbl[:, 1, :], ACT.Exp).then_inc(S["setup"], 1)

            @block.vector
            def _(dve):
                V = nc.vector
                ch = Chain(dve, S["fin"])
                dve.wait_ge(S["par_in"], BASE + 48)
                dve.wait_ge(S["const"], BASE + 8 + NL + 3 + NL + 1 + NL)
                V.tensor_tensor(lbl[:, 1, :], lbl[:, 0, :], lbl[:, 0, :], ALU.subtract).then_inc(S["setup"], 1)
                dve.wait_ge(S["setup"], BASE + 2)
                ch.link(V.reciprocal(lbl[:, 3, :], lbl[:, 2, :]))
                ch.link(V.tensor_tensor(lbl[:, 3, :], lbl[:, 3, :], lbl[:, 2, :], ALU.mult))
                ch.link(V.tensor_tensor(lbl[:, 3, :], lbl[:, 3, :], lbl[:, 3, :], ALU.subtract))
                ch.link(V.tensor_scalar(lbl[:, 1, :], lbl[:, 3, :], -1.0, 1.0, ALU.mult, ALU.add))
                for h in range(NH):
                    ch.link(V.tensor_scalar(heads(omf, P)[:, h, :], one[:, 0:P], lbl[:, 1, h:h + 1], None, ALU.mult))

        def each_step(eng, step):
            step(0, 0, 0, P, False, P)
            with eng.Fori(0, NTILE // 2 - 1) as i:
                for p in range(2):
                    step(2 * i + 1 + p, i + p, 1 - p, P, True, P)
            step(NTILE - 1, NTILE // 2 - 1, 1, P, True, NS)
            step(NTILE, NTILE // 2, 0, NS, True, 0)

        with nc.Block() as block:
            @block.sync
            def _(sp):
                def load_fg(p, t0, n):
                    sp.dma_start(heads(fc[p], n), zf[ZFC * P:(ZFC + NH) * P, t0].rearrange("(h p) t -> p h t", p=P)).then_inc(ld_fg[p], 16)
                    sp.dma_start(gc[p][:n, :], zt[t0, TGC:TGC + AW]).then_inc(ld_fg[p], 16)

                def load_q(p, t0, n):
                    sp.dma_start(heads(qr[p], n), zf[ZQC * P:(ZQC + NH) * P, t0].rearrange("(h p) t -> p h t", p=P)).then_inc(ld_q[p], 16)

                def load_v(p, t0, n):
                    sp.dma_start(vv[p][:n, :], zt[t0, TIC:TIC + AW]).then_inc(ld_v[p], 16)

                def turnover(it, p, n, n2):
                    if n2:
                        t2 = bass.ds((it + 2) * P, n2)
                        sp.wait_ge(S["q_ready"], BASE + it + 1)
                        load_q(p, t2, n2)
                        sp.wait_ge(S["gate_a"], BASE + it + 1)
                        load_fg(p, t2, n2)
                        sp.wait_ge(S["u_sum"], BASE + it + 3)
                        load_v(p, t2, n2)
                    sp.wait_ge(S["out"], BASE + it + 3)
                    sp.dma_start(mt[bass.ds(it * P, n), AW:2 * AW], oc[p][:n, :]).then_inc(ost[p], 16)

                for p in range(2):
                    load_fg(p, slice(p * P, (p + 1) * P), P)
                    load_q(p, slice(p * P, (p + 1) * P), P)
                    load_v(p, slice(p * P, (p + 1) * P), P)
                with sp.Fori(0, NTILE // 2 - 1) as i:
                    for p in range(2):
                        turnover(2 * i + p, p, P, P)
                turnover(NTILE - 2, 0, P, NS)
                turnover(NTILE - 1, 1, P, 0)
                sp.dma_start(io["hgrn_prompt"].rearrange("a h d v -> d (a h) v"),
                             state[:].rearrange("p (h v) -> p h v", v=HD)).then_inc(ost[1], 16)
                turnover(NTILE, 0, NS, 0)
                sp.dma_start(io["hgrn_sample"].rearrange("b h d v -> d (b h) v"),
                             s0[:].rearrange("p b (h v) -> p (b h) v", v=HD)).then_inc(ost[1], 16)
                sp.wait_ge(ost[0], BASE + 16 * (NTILE // 2 + 1))
                sp.wait_ge(ost[1], BASE + 16 * (NTILE // 2 + 2))

            @block.gpsimd
            def _(pool):
                G = nc.gpsimd

                def forget(it, p, n):
                    pool.wait_ge(S["sig"], BASE + 3 * it + 1)
                    G.tensor_tensor(heads(kk[p], n), heads(gg[p], n), heads(omf, P)[:, :, 0:n], ALU.mult).then_inc(S["gated"], 1)

                def output_gate(it, p, n):
                    pool.wait_ge(S["sig"], BASE + 3 * it + 3)
                    pool.wait_ge(S["out"], BASE + it + 1)
                    G.tensor_tensor(sg[p][:n, :], gsig[p][:n, :], gc[p][:n, :], ALU.mult).then_inc(S["gate_a"], 1)
                    pool.wait_ge(S["gate_a"], BASE + it + 1)
                    G.tensor_tensor(sg[p][:n, :], sg[p][:n, :], gnf[:n, :], ALU.mult).then_inc(S["gate_b"], 1)

                def power(it, p, n):
                    pool.wait_ge(S["stat"], BASE + 2 * it + 2)
                    G.tensor_tensor(small[p][:n, 2, :], small[p][:n, 1, :], con["mhalf"][:n, 0:1].to_broadcast([n, NH]),
                                    ALU.pow).then_inc(S["scaled"], 1)

                def step(it, i, p, n, prev, nxt):
                    w = NH * n
                    pool.wait_ge(S["b_ready"], BASE + it + 1)
                    seq = n if n == P else NT
                    b3 = bb[p][:, 0:w].rearrange("p (c w) -> p c w", w=seq)
                    last = b3[:, :, seq - 1:seq].to_broadcast([P, w // seq, seq])
                    pool.wait_ge(S["kd_turned"], BASE + it)
                    G.tensor_tensor(kd[p][:, 0:w].rearrange("p (c w) -> p c w", w=seq), last, b3,
                                    ALU.subtract).then_inc(S["dif_l"], 1)
                    for m, l in enumerate(levels(n)):
                        hs = HALVES[l]
                        b, d = blocks(bb[p], n, hs), blocks(lev[l], n, hs)
                        r = b[:, :, hs - 1:hs].to_broadcast([P, w // (2 * hs), hs])
                        pool.wait_ge(S["pairs"], BASE + NM * it + l + 2)
                        G.tensor_tensor(d[:, :, hs:], b[:, :, hs:], r, ALU.subtract)
                        G.tensor_tensor(d[:, :, :hs], r, b[:, :, :hs], ALU.subtract).then_inc(S["diff"], 1)
                    if nxt:
                        forget(it + 1, 1 - p, nxt)
                    output_gate(it, p, n)
                    if prev:
                        power(it - 1, 1 - p, P)

                forget(0, 0, P)
                each_step(pool, step)
                power(NTILE, 0, NS)

            @block.scalar
            def _(act):
                A = nc.scalar.activation

                def gate(it, i, p, n):
                    w = NH * n
                    act.wait_ge(ld_fg[p], BASE + 32 * i + 32)
                    act.wait_ge(S["gated"], BASE + max(it - 1, 0) if isinstance(it, int) else BASE + it - 1)
                    A(gg[p][:, 0:w], fc[p][:, 0:w], ACT.Sigmoid).then_inc(S["sig"], 1)
                    act.wait_ge(ld_q[p], BASE + 16 * i + 16)
                    A(sq[p][:, 0:w], qr[p][:, 0:w], ACT.Sigmoid).then_inc(S["sig"], 1)
                    A(gsig[p][:n, :], gc[p][:n, :], ACT.Sigmoid).then_inc(S["sig"], 1)
                    act.wait_ge(S["sig"], BASE + 3 * it + 1)
                    act.wait_ge(S["b_ready"], BASE + it)
                    for h in range(NH):
                        ins = A(heads(lg, n)[:, h, :], heads(gg[p], n)[:, h, :], ACT.Ln, bias=lbl[:, 3, h:h + 1], scale=lbl[:, 1, h:h + 1])
                    ins.then_inc(S["log_g"], 1)

                def square(it, n):
                    act.wait_ge(S["o_sum"], BASE + it + 1)
                    A(sqo[:n, :], op[:n, 0:AW], ACT.Square).then_inc(S["squared"], 1)

                def step(it, i, p, n, prev, nxt):
                    w = NH * n
                    act.wait_ge(S["dif_l"], BASE + it + 1)
                    A(kd[p][:, 0:w], kd[p][:, 0:w], ACT.Exp).then_inc(S["exp_l"], 1)
                    for m, l in enumerate(levels(n)):
                        act.wait_ge(S["diff"], BASE + NL * it + m + 1)
                        A(lev[l][:, 0:w], lev[l][:, 0:w], ACT.Exp).then_inc(S["expd"], 1)
                        if m == min(3, len(levels(n)) - 1) and prev:
                            square(it - 1, P)
                        if m == 0:
                            act.wait_ge(S["b_ready"], BASE + it + 1)
                            A(qd[p][:, 0:w], bb[p][:, 0:w], ACT.Exp).then_inc(S["exp_b"], 1)
                        if m == 1:
                            act.wait_ge(S["kd_turned"], BASE + it + 2)
                            A(kdt[p][:n, :], tp[:n, 0:W], ACT.Copy).then_inc(S["kd_copied"], 1)
                    if nxt:
                        gate(it + 1, i + p, 1 - p, nxt)

                gate(0, 0, 0, P)
                each_step(act, step)
                square(NTILE, NS)

            @block.vector
            def _(dve):
                V = nc.vector
                dve.sem_inc(S["out"], 2)
                v3 = lambda t: t.rearrange("p (h v) -> p h v", v=HD)

                def query_key(it, p, n):
                    w = NH * n
                    dve.wait_ge(S["sig"], BASE + 3 * it + 2)
                    V.scalar_tensor_tensor(out=qc[p][:, 0:w], in0=qr[p][:, 0:w], scalar=float(P) ** -0.5,
                                           in1=sq[p][:, 0:w], op0=ALU.mult, op1=ALU.mult).then_inc(S["q_ready"], 1)
                    dve.wait_ge(S["gated"], BASE + it + 1)
                    V.tensor_tensor(heads(kk[p], n), heads(omf, P)[:, :, 0:n], heads(kk[p], n), ALU.subtract).then_inc(S["k_ready"], 1)

                def scan(it, p, n):
                    dve.wait_ge(S["log_g"], BASE + it + 1)
                    V.tensor_tensor_scan(bb[p][:, 0:NH * n], (cut if n == P else cut_s)[:, 0:NH * n], lg[:, 0:NH * n], 0.0,
                                         ALU.mult, ALU.add).then_inc(S["b_ready"], 1)

                def decayed_query(it, p, n):
                    w = NH * n
                    dve.wait_ge(S["exp_b"], BASE + it + 1)
                    dve.wait_ge(S["q_ready"], BASE + it + 1)
                    if n == P:
                        V.tensor_copy(glast[p][:], heads(qd[p], n)[:, :, n - 1]).then_inc(S["g_last"], 1)
                        dve.wait_ge(S["g_last"], BASE + it + 1)
                        V.tensor_tensor(qd[p][:, 0:w], qd[p][:, 0:w], qc[p][:, 0:w], ALU.mult).then_inc(S["qd_ready"], 1)
                    else:
                        gl = s_gl[:].rearrange("p (b h) -> p h b", h=NH)
                        V.tensor_copy(gl, qd[p][:, 0:w].rearrange("p (h b t) -> p h b t", h=NH, t=NT)[:, :, :, NT - 1]).then_inc(S["g_last"], 1)
                        dve.wait_ge(S["g_last"], BASE + it + 1)
                        dve.wait_ge(ld_v[p], BASE + 16 * (NTILE // 2 + 1))
                        for b in range(NB):
                            cols = slice(b * NT, (b + 1) * NT)
                            V.tensor_tensor(qdb[:, b, :].rearrange("p (h t) -> p h t", h=NH)[:, :, cols],
                                            heads(qd[p], n)[:, :, cols], heads(qc[p], n)[:, :, cols], ALU.mult).then_inc(S["qdb_r"], 1)
                            V.tensor_scalar(vb[:, b, :], vv[p][:n, :], rowm[:, b:b + 1], None, ALU.mult).then_inc(S["vb_r"], 1)

                def new_state(it, p):
                    dve.wait_ge(S["o_sum"], BASE + it + 1)
                    V.tensor_tensor(v3(stmp[:]), v3(state[:]), glast[p][:].unsqueeze(2).to_broadcast([P, NH, HD]),
                                    ALU.mult).then_inc(S["s_tmp"], 1)
                    dve.wait_ge(S["s_tmp"], BASE + it + 1)
                    dve.wait_ge(S["u_sum"], BASE + it + 3)
                    V.tensor_tensor(state[:], stmp[:], up[:, 0:AW], ALU.add).then_inc(S["s_new"], 1)

                def statistics(it, p, n):
                    dve.wait_ge(S["squared"], BASE + it + 1)
                    V.reduce_sum(small[p][:n, 0, :], v3(sqo[:n, :]), AX_X).then_inc(S["stat"], 1)
                    dve.wait_ge(S["stat"], BASE + 2 * it + 1)
                    V.tensor_scalar(small[p][:n, 1, :], small[p][:n, 0, :], 1.0 / HD, EPS, ALU.mult, ALU.add).then_inc(S["stat"], 1)

                def output(it, i, p, n):
                    dve.wait_ge(S["scaled"], BASE + it + 1)
                    dve.wait_ge(ost[p], BASE + 16 * i)
                    V.tensor_tensor(v3(oc[p][:n, :]), v3(op[:n, 0:AW]),
                                    small[p][:n, 2, :].unsqueeze(2).to_broadcast([n, NH, HD]), ALU.mult).then_inc(S["normed"], 1)
                    dve.wait_ge(S["normed"], BASE + it + 1)
                    dve.wait_ge(S["gate_b"], BASE + it + 1)
                    V.tensor_tensor(oc[p][:n, :], oc[p][:n, :], sg[p][:n, :], ALU.mult).then_inc(S["out"], 1)

                def step(it, i, p, n, prev, nxt):
                    w = NH * n

                    def take(j):
                        dve.wait_ge(S["pairs"], BASE + NM * it + NM + j + 1)
                        if j:
                            dve.wait_ge(S["taken"], BASE + NM * it + j)
                        m = mask[levels(n)[j - 1]] if j else con["ident"]
                        hold(dve, S["held"])
                        V.copy_predicated((attn[p] if n == P else attn_s)[:n, :, :n], m[:n, 0:n].bitcast(I32).unsqueeze(1).to_broadcast([n, NH, n]),
                                          lp[j % 2][:n, 0:w].rearrange("p (h t) -> p h t", h=NH)).then_inc(S["taken"], 1)

                    dve.wait_ge(S["k_ready"], BASE + it + 1)
                    dve.wait_ge(S["exp_l"], BASE + it + 1)
                    V.tensor_tensor(kd[p][:, 0:w], kd[p][:, 0:w], kk[p][:, 0:w], ALU.mult).then_inc(S["kd_ready"], 1)
                    L = len(levels(n))
                    for m, l in enumerate(levels(n)):
                        hs = HALVES[l]
                        dve.wait_ge(S["expd"], BASE + NL * it + m + 1)
                        e, q3, k3 = (blocks(t, n, hs) for t in (lev[l], qc[p], kk[p]))
                        V.tensor_tensor(e[:, :, hs:], e[:, :, hs:], q3[:, :, hs:], ALU.mult)
                        V.tensor_tensor(e[:, :, :hs], e[:, :, :hs], k3[:, :, :hs], ALU.mult).then_inc(S["xlev"], 1)
                        take(m)
                        if m == 1:
                            decayed_query(it, p, n)
                        if m == min(3, L - 1) and prev:
                            new_state(it - 1, 1 - p)
                        if m == min(4, L - 1) and prev:
                            statistics(it - 1, 1 - p, P)
                        if m == 5 and nxt:
                            scan(it + 1, 1 - p, nxt)
                    if nxt:
                        query_key(it + 1, 1 - p, nxt)
                    if prev:
                        output(it - 1, i - 1 + p, 1 - p, P)
                    take(len(levels(n)))

                scan(0, 0, P)
                query_key(0, 0, P)
                each_step(dve, step)
                dve.wait_ge(S["o_sum"], BASE + NTILE + 1)
                for b in range(NB):
                    V.tensor_tensor(v3(s0[:, b, :]), v3(s0[:, b, :]), s_gl[:, b * NH:(b + 1) * NH].unsqueeze(2).to_broadcast([P, NH, HD]),
                                    ALU.mult).then_inc(S["s_tmp"], 1)
                    dve.wait_ge(S["s_tmp"], BASE + NTILE + b + 1)
                    dve.wait_ge(S["us"], BASE + b + 1)
                    V.tensor_tensor(s0[:, b, :], s0[:, b, :], ub[b % 2][:, 0:AW], ALU.add).then_inc(S["s_new"], 1)
                statistics(NTILE, 0, NS)
                output(NTILE, NTILE // 2, 0, NS)

            @block.tensor
            def _(pe):
                pe.sem_inc(S["pairs"], NM)
                pe.sem_inc(S["kd_turned"], 1)
                pe.sem_inc(S["u_sum"], 2)
                hv = lambda h: slice(h * HD, (h + 1) * HD)

                def outputs(it, i, p, n):
                    pe.wait_ge(S["taken"], BASE + NM * it + 1 + len(levels(n)))
                    pe.wait_ge(ld_v[p], BASE + 16 * i + 16)
                    pe.wait_ge(S["out"], BASE + it + 2)
                    if n == P:
                        pe.wait_ge(S["s_new"], BASE + it)
                        pe.wait_ge(S["qd_ready"], BASE + it + 1)
                    else:
                        pe.wait_ge(S["qdb_r"], BASE + NB)
                        pe.wait_ge(S["vb_r"], BASE + NB)
                    for h in range(NH):
                        nc.tensor.matmul(op[:n, hv(h)], (attn[p] if n == P else attn_s)[:n, h, :n], vv[p][:n, hv(h)], start=True, stop=False)
                        if n == P:
                            mm = nc.tensor.matmul(op[:n, hv(h)], qd[p][:, h * n:(h + 1) * n], state[:, hv(h)], start=False, stop=True)
                        else:
                            for b in range(NB):
                                mm = nc.tensor.matmul(op[:n, hv(h)], qdb[:, b, h * n:(h + 1) * n], s0[:, b, hv(h)],
                                                      start=False, stop=(b == NB - 1))
                    mm.then_inc(S["o_sum"], 1)
                    if n == P:
                        pe.wait_ge(S["kd_copied"], BASE + it + 1)
                        for h in range(NH):
                            mm = nc.tensor.matmul(up[:, hv(h)], kdt[p][:n, h * P:(h + 1) * P], vv[p][:n, hv(h)], start=True, stop=True)
                        mm.then_inc(S["u_sum"], 1)

                def step(it, i, p, n, prev, nxt):
                    def pairs(j, left, right):
                        if j >= 2:
                            pe.wait_ge(S["taken"], BASE + NM * it + j - 1)
                        elif prev:
                            pe.wait_ge(S["taken"], BASE + NM * it)
                        for h in range(NH):
                            cols = slice(h * n, (h + 1) * n)
                            mm = nc.tensor.matmul(lp[j % 2][:n, cols], left[:, cols], right[:, cols], start=True, stop=True)
                        mm.then_inc(S["pairs"], 1)

                    pe.wait_ge(S["q_ready"], BASE + it + 1)
                    pe.wait_ge(S["k_ready"], BASE + it + 1)
                    pairs(0, kk[p], qc[p])
                    pe.wait_ge(S["kd_ready"], BASE + it + 1)
                    pe.wait_ge(S["kd_copied"], BASE + it)
                    for h in range(NH):
                        mm = nc.tensor.transpose(tp[:n, h * P:(h + 1) * P], kd[p][:, h * n:(h + 1) * n], con["ident"][:, :])
                    mm.then_inc(S["kd_turned"], 1)
                    for m, l in enumerate(levels(n)):
                        pe.wait_ge(S["xlev"], BASE + NL * it + m + 1)
                        pairs(m + 1, lev[l], lev[l])
                        if m == 1 and prev:
                            outputs(it - 1, i - 1 + p, 1 - p, P)

                each_step(pe, step)
                outputs(NTILE, NTILE // 2, 0, NS)
                pe.wait_ge(S["kd_copied"], BASE + NTILE + 1)
                for b in range(NB):
                    pe.wait_ge(S["s_new"], BASE + NTILE + max(b - 1, 0))
                    for h in range(NH):
                        mm = nc.tensor.matmul(ub[b % 2][:, hv(h)], kdt[0][:NS, h * P:(h + 1) * P], vb[:, b, hv(h)],
                                              start=True, stop=True)
                    mm.then_inc(S["us"], 1)


def multiplicity_mask(V, link, d, low, cnt, out):
    V_ts, V_stt = V.tensor_scalar, V.scalar_tensor_tensor
    (w1, r1), (w2, r2), (w3, r3) = DILATED
    link(V_ts(low, d, r2 - 1, None, ALU.bitwise_and))
    link(V_ts(out, low, 0.0, None, ALU.is_equal))
    link(V_stt(out=out, in0=d, scalar=float(w2), in1=out, op0=ALU.is_le, op1=ALU.mult))
    link(V_stt(out=out, in0=d, scalar=float(w1), in1=out, op0=ALU.is_le, op1=ALU.add))
    link(V_ts(low, d, r3 - 1, None, ALU.bitwise_and))
    link(V_ts(cnt, low, 0.0, None, ALU.is_equal))
    link(V_stt(out=cnt, in0=d, scalar=float(w3), in1=cnt, op0=ALU.is_le, op1=ALU.mult))
    link(V.tensor_tensor(cnt, cnt, out, ALU.add))
    link(V_stt(out=cnt, in0=d, scalar=0.0, in1=cnt, op0=ALU.is_ge, op1=ALU.mult))
    link(V_ts(out, cnt, 0.0, NEG, ALU.is_equal, ALU.mult))
    for k in (2, 3):
        link(V_ts(low.bitcast(F32), cnt, float(k), float(np.log(k)) / SCALE, ALU.is_equal, ALU.mult))
        link(V.tensor_tensor(out, out, low.bitcast(F32), ALU.add))


def attend_prompt(nc, sem, io, con, zf, zt, mt):
    with ExitStack() as ctx:
        def sb(name, shape, dt=F32):
            return ctx.enter_context(nc.sbuf_tensor("a_" + name, shape, dt))

        two = lambda name, shape, dt=F32: [sb(f"{name}{p}", shape, dt) for p in range(2)]
        q2, k2 = two("q2", [P, SEQ]), two("k2", [P, SEQ])
        vv, ga = two("vv", [P, NTILE, HD]), two("ga", [P, NTILE, HD])
        oa = two("oa", [P, NTILE, HD])
        khi, klo, qst = two("khi", [P, SEQ], F32R), two("klo", [P, SEQ], F32R), two("qst", [P, SEQ], F32R)
        qhi = sb("qhi", [P, SEQ], F32R)
        prob = two("prob", [P, SEQ])
        pt = [sb(f"pt{r}", [P, 4 * P]) for r in range(4)]
        gs = sb("gs", [P, NTILE, HD])
        mask = sb("mask", [P, SEQ])
        stat = sb("stat", [P, 3, NTILE])
        sp_ = ctx.enter_context(nc.psum_tensor("a_s", [P, SEQ], F32))
        tp = [ctx.enter_context(nc.psum_tensor(f"a_t{b}", [P, 512], F32)) for b in range(2)]
        op = [ctx.enter_context(nc.psum_tensor(f"a_o{b}", [P, 512], F32)) for b in range(2)]
        ld = [sem(f"a_ld{p}") for p in range(2)]
        st_ = [sem(f"a_store{p}") for p in range(2)]
        windows = sem("a_windows")
        S = {n: sem("a_" + n) for n in ("iota", "mask", "hi", "split", "sig", "silu", "scores", "shifted", "exped",
                                        "turned", "copied_a", "copied_v", "o_sum", "recip", "final", "held")}
        groups = [[list(range(m, min(m + 4, n + 1))) for m in range(0, n + 1, 4)] for n in range(NTILE)]
        first = [sum(len(g) for g in groups[:n]) for n in range(NTILE + 1)]
        NG = first[-1]
        owner = ["v" if j + 1 == first[n + 1] and n % 4 > 0 else "a" for n in range(NTILE) for j in range(first[n], first[n + 1])]

        def copied(pe, it, j):
            mine = owner[j % NG]
            count = owner[:j + 1].count(mine) if j >= 0 else 0
            pe.wait_ge(S["copied_" + mine], BASE + owner.count(mine) * it + count)

        with nc.Block() as block:
            @block.gpsimd
            def _(pool):
                nc.gpsimd.iota(prob[0][:].bitcast(I32), pattern=[[-1, SEQ]], base=SEQ - P, channel_multiplier=1).then_inc(S["iota"], 1)

            @block.vector
            def _(dve):
                dve.wait_ge(S["iota"], BASE + 1)
                multiplicity_mask(nc.vector, Chain(dve, S["mask"]).link, prob[0][:].bitcast(I32), prob[1][:].bitcast(I32), q2[0][:], mask[:])

        with nc.Block() as block:
            def per_head(eng, body):
                with eng.Fori(0, NH // 2) as i:
                    for p in range(2):
                        body(2 * i + p, i, p)

            def per_head_ahead(eng, body):
                with eng.Fori(0, NH // 2 - 1) as i:
                    for p in range(2):
                        body(2 * i + p, i, p, True)
                for p in range(2):
                    body(NH - 2 + p, NH // 2 - 1, p, p == 0)

            @block.sync
            def _(sp):
                def load(it, p):
                    for d in range(2):
                        rows = slice(d * HD, (d + 1) * HD)
                        sp.dma_start(q2[p][rows, :], zf[bass.ds(it * HD + ZQ * P, HD), 0:SEQ]).then_inc(ld[p], 16)
                        sp.dma_start(k2[p][rows, :], zf[bass.ds(it * HD + ZK * P, HD), 0:SEQ]).then_inc(ld[p], 16)
                    for t, c in ((vv, TV), (ga, TGA)):
                        sp.dma_start(t[p][:], zt[0:SEQ, bass.ds(it * HD + c, HD)].rearrange("(n p) d -> p n d", p=P)).then_inc(ld[p], 16)

                def save(it, p):
                    sp.wait_ge(S["final"], BASE + NTILE * it + 2 * NTILE)
                    sp.dma_start(mt[0:SEQ, bass.ds(it * HD, HD)].rearrange("(n p) d -> p n d", p=P), oa[p][:]).then_inc(st_[p], 16)

                for p in range(2):
                    load(p, p)
                for name, rows, col in (("k_win_prompt", slice(0, SEQ), TK), ("v_win_prompt", slice(0, SEQ), TV),
                                        ("k_win_sample", slice(SEQ, T), TK), ("v_win_sample", slice(SEQ, T), TV)):
                    if name in io:
                        sp.dma_start(io[name], zt[rows, col:col + AW]).then_inc(windows, 16)
                with sp.Fori(0, NH // 2 - 1) as i:
                    for p in range(2):
                        save(2 * i + p, p)
                        load(2 * i + p + 2, p)
                for p in range(2):
                    save(NH - 2 + p, p)
                for p in range(2):
                    sp.wait_ge(st_[p], BASE + 16 * NH // 2)
                if "k_win_prompt" in io:
                    sp.wait_ge(windows, BASE + 64)

            @block.gpsimd
            def _(pool):
                def body(it, i, p):
                    pool.wait_ge(S["sig"], BASE + it + 1)
                    nc.gpsimd.tensor_tensor(ga[p][:], ga[p][:], gs[:], ALU.mult).then_inc(S["silu"], 1)

                per_head(pool, body)

            def copies(eng, it, n, mine):
                for g, blocks in enumerate(groups[n]):
                    j = first[n] + g
                    if owner[j] != mine:
                        continue
                    w = len(blocks) * P
                    eng.wait_ge(S["turned"], BASE + NG * it + j + 1)
                    eng.wait_ge(S["o_sum"], BASE + NG * it + max(j - 3, 0))
                    if mine == "a":
                        nc.scalar.activation(pt[j % 4][:, :w], tp[j % 2][:, :w], ACT.Copy).then_inc(S["copied_a"], 1)
                    else:
                        nc.vector.tensor_copy(pt[j % 4][:, :w], tp[j % 2][:, :w]).then_inc(S["copied_v"], 1)

            @block.scalar
            def _(act):
                A = nc.scalar.activation

                def sigmoid(it, i, p):
                    act.wait_ge(ld[p], BASE + 96 * i + 96)
                    act.wait_ge(S["silu"], BASE + it)
                    A(gs[:], ga[p][:], ACT.Sigmoid).then_inc(S["sig"], 1)

                def body(it, i, p, ahead):
                    for n in range(NTILE + 1):
                        if n == NTILE // 2 and ahead:
                            sigmoid(it + 1, i + p, 1 - p)
                        if n:
                            copies(act, it, n - 1, "a")
                        if n < NTILE:
                            w = (n + 1) * P
                            act.wait_ge(S["shifted"], BASE + NTILE * it + n + 1)
                            A(prob[n % 2][:, :w], prob[n % 2][:, :w], ACT.Exp, bias=stat[:, 0, n:n + 1], scale=-1.0,
                              accum_out=stat[:, 1, n:n + 1]).then_inc(S["exped"], 1)

                sigmoid(0, 0, 0)
                per_head_ahead(act, body)

            @block.vector
            def _(dve):
                V = nc.vector
                dve.sem_inc(S["final"], NTILE)

                def split(it, i, p, part):
                    if part == 0:
                        dve.wait_ge(ld[p], BASE + 96 * i + 96)
                        V.tensor_copy(khi[p][:], k2[p][:]).then_inc(S["hi"], 1)
                    elif part == 1:
                        V.tensor_copy(qhi[:], q2[p][:]).then_inc(S["hi"], 1)
                    elif part == 2:
                        dve.wait_ge(S["hi"], BASE + 2 * it + 2)
                        V.tensor_tensor(klo[p][:], k2[p][:], khi[p][:], ALU.subtract).then_inc(S["split"], 1)
                    elif part == 3:
                        V.tensor_copy(qst[p][:HD, :], q2[p][:HD, :]).then_inc(S["split"], 1)
                    elif part == 4:
                        V.tensor_tensor(qst[p][HD:, :], q2[p][HD:, :], qhi[HD:, :], ALU.subtract).then_inc(S["split"], 1)

                def body(it, i, p, ahead):
                    dve.wait_ge(st_[p], BASE + 16 * i)
                    dve.wait_ge(S["silu"], BASE + it + 1)
                    for n in range(NTILE + 2):
                        if n < NTILE:
                            w = (n + 1) * P
                            dve.wait_ge(S["scores"], BASE + NTILE * it + n + 1)
                            if n >= 2:
                                dve.wait_ge(S["turned"], BASE + NG * it + first[n - 1])
                            hold(dve, S["held"])
                            V.tensor_tensor_reduce(out=prob[n % 2][:, :w], in0=sp_[:, :w], in1=mask[:, SEQ - w:],
                                                   scale=-SCALE, scalar=1.0e30, op0=ALU.add, op1=ALU.min,
                                                   accum_out=stat[:, 0, n:n + 1]).then_inc(S["shifted"], 1)
                        if 1 <= n <= NTILE:
                            copies(dve, it, n - 1, "v")
                        if ahead and n >= NTILE // 2:
                            split(it + 1, i + p, 1 - p, n - NTILE // 2)
                        if n >= 2:
                            m = n - 2
                            dve.wait_ge(S["exped"], BASE + NTILE * it + m + 1)
                            V.reciprocal(stat[:, 2, m:m + 1], stat[:, 1, m:m + 1]).then_inc(S["recip"], 1)
                            dve.wait_ge(S["recip"], BASE + NTILE * it + m + 1)
                            dve.wait_ge(S["o_sum"], BASE + NG * it + first[m + 1])
                            V.scalar_tensor_tensor(out=oa[p][:, m, :], in0=op[m % 2][:, :HD], scalar=stat[:, 2, m:m + 1],
                                                   in1=ga[p][:, m, :], op0=ALU.mult, op1=ALU.mult).then_inc(S["final"], 1)

                for part in range(5):
                    split(0, 0, 0, part)
                per_head_ahead(dve, body)

            @block.tensor
            def _(pe):
                def body(it, i, p):
                    pe.wait_ge(S["split"], BASE + 3 * it + 3)
                    for n in range(NTILE + 1):
                        if n < NTILE:
                            if n:
                                pe.wait_ge(S["shifted"], BASE + NTILE * it + n)
                            for c in range(0, (n + 1) * P, 512):
                                w = min(512, (n + 1) * P - c)
                                q = qst[p][:, n * P:(n + 1) * P]
                                nc.tensor.matmul(sp_[:, c:c + w], q, khi[p][:, c:c + w], start=True, stop=False)
                                mm = nc.tensor.matmul(sp_[:, c:c + w], q, klo[p][:, c:c + w], start=False, stop=True)
                            mm.then_inc(S["scores"], 1)
                        if n:
                            m = n - 1
                            pe.wait_ge(S["exped"], BASE + NTILE * it + m + 1)
                            for g in range(len(groups[m]) + 1):
                                if g < len(groups[m]):
                                    j = first[m] + g
                                    copied(pe, it, j - 2)
                                    for c, b in enumerate(groups[m][g]):
                                        mm = nc.tensor.transpose(tp[j % 2][:, c * P:(c + 1) * P], prob[m % 2][:, b * P:(b + 1) * P],
                                                                 con["ident"][:, :])
                                    mm.then_inc(S["turned"], 1)
                                if g:
                                    j = first[m] + g - 1
                                    if g == 1:
                                        pe.wait_ge(S["final"], BASE + NTILE * it + NTILE + max(m - 1, 0))
                                    copied(pe, it, j)
                                    for c, b in enumerate(groups[m][g - 1]):
                                        mm = nc.tensor.matmul(op[m % 2][:, :HD], pt[j % 4][:, c * P:(c + 1) * P], vv[p][:, b, :],
                                                              start=(b == 0), stop=(b == m))
                                    mm.then_inc(S["o_sum"], 1)

                per_head(pe, body)


def attend_sample(nc, sem, io, con, zf, zt, mt):
    NEAR = 512
    FAR = WIN - NEAR
    (_, _), (_, _), (w3, r3) = DILATED
    NFAR = FAR // r3 * NT
    KT = (NFAR + NEAR) // P
    NK = NFAR + NEAR + NT
    R = NH * NT
    width = [P] * KT + [NT]
    with ExitStack() as ctx:
        def sb(name, shape, dt=F32):
            return ctx.enter_context(nc.sbuf_tensor("s_" + name, shape, dt))

        two = lambda name, shape, dt=F32: [sb(f"{name}{p}", shape, dt) for p in range(2)]
        kk, vv = two("k", [P, KT + 1, AW]), two("v", [P, KT + 1, AW])
        kt = sb("kt", [P, 3, NK])
        qs, qbd = sb("qs", [P, 3, NS]), sb("qbd", [P, NB, 3 * R])
        qcur = two("qcur", [P, 3 * R])
        prob = two("prob", [R, NK])
        ptt = two("ptt", [P, KT + 1, R])
        mask, cnt, dist = sb("mask", [R, NK]), sb("cnt", [R, NK]), sb("dist", [R, 2, NK], I32)
        tcol = sb("tcol", [R, 2], I32)
        tf = sb("tf", [R, 1])
        stat = two("stat", [R, 4])
        orow = sb("orow", [2 * NT, AW])
        ot, os_ = sb("ot", [P, 3, NS]), sb("os", [NS, AW])
        ga, gs = sb("ga", [NS, AW]), sb("gs", [NS, AW])
        sp_ = ctx.enter_context(nc.psum_tensor("s_s", [P, 1536], F32))
        tp = [ctx.enter_context(nc.psum_tensor(f"s_t{b}", [P, 512], F32)) for b in range(2)]
        pp = ctx.enter_context(nc.psum_tensor("s_p", [P, 1024], F32))
        op = ctx.enter_context(nc.psum_tensor("s_o", [P, 512], F32))
        ld = [sem(f"s_ld{p}") for p in range(2)]
        S = {n: sem("s_" + n) for n in ("par_in", "made", "mask", "qbd", "q_cur", "k_turned", "copied_a", "copied_v", "scores",
                                        "shifted", "exped", "recip", "normed", "p_turned", "p_copied", "o_sum", "gathered",
                                        "sig", "gate", "o_turned", "final", "store", "upper", "o_rows", "rows_out", "held_v", "held_t")}
        groups = [(pr, a, min(a + 4, KT + 1)) for a in range(0, KT + 1, 4) for pr in range(3)]
        NG = len(groups)
        ODD, EVEN = NG // 2, (NG + 1) // 2
        at = lambda n: sum(width[:n])
        PB = 8

        with nc.Block() as block:
            def load(sp, it, p):
                for t, cache, c in ((kk, io["ck"], TK), (vv, io["cv"], TV)):
                    for j in range(NFAR // P):
                        m = P // NT * r3
                        src = cache[bass.ds(it, 1), j * m:(j + 1) * m, :].rearrange("b (m r) c -> (b m) r c", r=r3)[:, 0:NT, :]
                        sp.dma_start(t[p][:, j, :], src).then_inc(ld[p], 16)
                    src = cache[bass.ds(it, 1), FAR:WIN, :].rearrange("b (n p) c -> p (b n) c", p=P)
                    sp.dma_start(t[p][:, NFAR // P:KT, :], src).then_inc(ld[p], 16)
                    sp.dma_start(t[p][:NT, KT, :], zt[bass.ds(it * NT + SEQ, NT), c:c + AW]).then_inc(ld[p], 16)

            @block.sync
            def _(sp):
                sp.dma_start(qs[:], zf[ZQ * P:(ZQ + 3) * P, SEQ:T].rearrange("(c p) t -> p c t", p=P)).then_inc(S["par_in"], 16)
                sp.dma_start(ga[:], zt[SEQ:T, TGA:TGA + AW]).then_inc(S["par_in"], 16)
                for p in range(2):
                    load(sp, p, p)

            @block.gpsimd
            def _(pool):
                G = nc.gpsimd
                G.iota(tcol[:, 0:1], pattern=[[0, 1]], base=0, channel_multiplier=1).then_inc(S["made"], 1)
                G.memset(qbd[:], 0.0).then_inc(S["made"], 1)
                G.iota(dist[:, 0, 0:NFAR], pattern=[[-r3, FAR // r3], [-1, NT]], base=WIN, channel_multiplier=0).then_inc(S["made"], 1)
                G.iota(dist[:, 0, NFAR:NK], pattern=[[-1, NEAR + NT]], base=NEAR, channel_multiplier=0).then_inc(S["made"], 1)
                pool.wait_ge(S["made"], BASE + 4)

            @block.vector
            def _(dve):
                V = nc.vector
                ch = Chain(dve, S["mask"])
                dve.wait_ge(S["made"], BASE + 4)
                dve.wait_ge(S["par_in"], BASE + 32)
                ch.link(V.tensor_scalar(tcol[:, 1:2], tcol[:, 0:1], NT - 1, None, ALU.bitwise_and))
                ch.link(V.tensor_copy(tf[:], tcol[:, 1:2]))
                ch.link(V.tensor_scalar(dist[:, 1, :], dist[:, 0, :], tf[:, 0:1], None, ALU.add))
                multiplicity_mask(V, ch.link, dist[:, 1, :], dist[:, 0, :], cnt[:], mask[:])
                for hp in range(2):
                    rows = slice(hp * HD, (hp + 1) * HD)
                    for pr in range(3):
                        h = 2 * pr + hp
                        dst = qbd[rows, :, pr * R + h * NT:pr * R + (h + 1) * NT]
                        ch.link(V.tensor_copy(dst, qs[rows, pr, :].rearrange("p (b t) -> p b t", t=NT)))

        with nc.Block() as block:
            def per_sample(eng, body):
                with eng.Fori(0, NB // 2) as i:
                    for p in range(2):
                        body(2 * i + p, i, p)

            @block.sync
            def _(sp):
                with sp.Fori(1, NB // 2) as i:
                    for p in range(2):
                        sp.wait_ge(S["gathered"], BASE + 2 * i + p + 1)
                        load(sp, 2 * i + p, p)
                sp.wait_ge(S["final"], BASE + 1)
                sp.dma_start(mt[SEQ:T, 0:AW], os_[:]).then_inc(S["store"], 16)
                sp.wait_ge(S["store"], BASE + 16)

            LOADS = 16 * 2 * (NFAR // P + 2)

            def copies(eng, it, odd):
                for j, (pr, a, b) in enumerate(groups):
                    if j % 2 != odd:
                        continue
                    w = at(b) - at(a)
                    eng.wait_ge(S["k_turned"], BASE + NG * it + j + 1)
                    eng.wait_ge(S["scores"], BASE + 3 * it)
                    dst = kt[:, pr, at(a):at(b)]
                    if odd:
                        nc.scalar.activation(dst, tp[1][:, :w], ACT.Copy).then_inc(S["copied_a"], 1)
                    else:
                        nc.vector.tensor_copy(dst, tp[0][:, :w]).then_inc(S["copied_v"], 1)

            @block.scalar
            def _(act):
                A = nc.scalar.activation
                A(gs[:], ga[:], ACT.Sigmoid).then_inc(S["sig"], 1)

                def body(it, i, p):
                    copies(act, it, 1)
                    act.wait_ge(S["shifted"], BASE + it + 1)
                    A(prob[p][:, :], prob[p][:, :], ACT.Exp, bias=stat[p][:, 0:1], scale=-1.0,
                      accum_out=stat[p][:, 1:2]).then_inc(S["exped"], 1)
                    act.wait_ge(S["p_turned"], BASE + it + 1)
                    A(ptt[p][:, 0:PB, :], pp[:, 0:PB * R].rearrange("p (n r) -> p n r", r=R), ACT.Copy).then_inc(S["p_copied"], 1)
                    A(ptt[p][:, PB:KT, :], pp[:, 512:512 + (KT - PB) * R].rearrange("p (n r) -> p n r", r=R), ACT.Copy).then_inc(S["p_copied"], 1)
                    A(ptt[p][:NT, KT, :], pp[:NT, 512 + (KT - PB) * R:512 + (KT - PB + 1) * R], ACT.Copy).then_inc(S["p_copied"], 1)

                per_sample(act, body)

            @block.vector
            def _(dve):
                V = nc.vector
                dve.sem_inc(S["gathered"], 2)
                dve.wait_ge(S["sig"], BASE + 1)
                V.tensor_tensor(ga[:], ga[:], gs[:], ALU.mult).then_inc(S["gate"], 1)

                def body(it, i, p):
                    V.tensor_copy(qcur[p][:], qbd[:, bass.ds(it, 1), :].rearrange("p b c -> p (b c)")).then_inc(S["q_cur"], 1)
                    copies(dve, it, 0)
                    dve.wait_ge(S["scores"], BASE + 3 * it + 3)
                    hold(dve, S["held_v"])
                    V.tensor_tensor_reduce(out=prob[p][:, :], in0=sp_[:R, :NK], in1=mask[:], scale=-SCALE, scalar=1.0e30,
                                           op0=ALU.add, op1=ALU.min, accum_out=stat[p][:, 0:1]).then_inc(S["shifted"], 1)
                    dve.wait_ge(S["exped"], BASE + it + 1)
                    V.reciprocal(stat[p][:, 2:3], stat[p][:, 1:2]).then_inc(S["recip"], 1)
                    dve.wait_ge(S["recip"], BASE + it + 1)
                    V.tensor_scalar(prob[p][:, :], prob[p][:, :], stat[p][:, 2:3], None, ALU.mult).then_inc(S["normed"], 1)
                    dve.wait_ge(S["o_rows"], BASE + it + 1)
                    V.tensor_copy(orow[:], op[:2 * NT, 0:AW]).then_inc(S["rows_out"], 1)
                    dve.wait_ge(S["o_sum"], BASE + it + 1)
                    o3 = op[:, AW:AW + 3 * 2 * NT].rearrange("p (c x) -> p c x", c=3)
                    cols = bass.ds(it * NT, NT)
                    V.tensor_copy(ot[0:HD, :, cols], o3[0:HD, :, 0:NT]).then_inc(S["upper"], 1)
                    V.tensor_copy(ot[HD:P, :, cols], o3[HD:P, :, NT:2 * NT]).then_inc(S["gathered"], 1)

                per_sample(dve, body)
                dve.wait_ge(S["o_turned"], BASE + 1)
                dve.wait_ge(S["gate"], BASE + 1)
                V.tensor_tensor(os_[:], tp[0][:NS, 0:AW], ga[:], ALU.mult).then_inc(S["final"], 1)

            @block.tensor
            def _(pe):
                def body(it, i, p):
                    pe.wait_ge(ld[p], BASE + LOADS * i + LOADS)
                    pe.wait_ge(S["q_cur"], BASE + it + 1)
                    def score(c):
                        for j in (3 * c + 1, 3 * c + 2):
                            if j % 2:
                                pe.wait_ge(S["copied_a"], BASE + ODD * it + j // 2 + 1)
                            else:
                                pe.wait_ge(S["copied_v"], BASE + EVEN * it + j // 2 + 1)
                        w = min(512, NK - 512 * c)
                        for pr in range(3):
                            mm = nc.tensor.matmul(sp_[:R, 512 * c:512 * c + w], qcur[p][:, pr * R:(pr + 1) * R],
                                                  kt[:, pr, 512 * c:512 * c + w], start=(pr == 0), stop=(pr == 2))
                        mm.then_inc(S["scores"], 1)

                    for j, (pr, a, b) in enumerate(groups):
                        if j % 2:
                            pe.wait_ge(S["copied_a"], BASE + ODD * it + j // 2)
                        else:
                            pe.wait_ge(S["copied_v"], BASE + EVEN * it + j // 2)
                        for n in range(a, b):
                            o = at(n) - at(a)
                            mm = nc.tensor.transpose(tp[j % 2][:, o:o + width[n]], kk[p][:width[n], n, pr * P:(pr + 1) * P],
                                                     con["ident"][:width[n], :width[n]])
                        mm.then_inc(S["k_turned"], 1)
                        if j % 3 == 2 and j > 3:
                            if j == 5:
                                pe.wait_ge(S["shifted"], BASE + it)
                            score(j // 3 - 1)
                    score(NG // 3 - 1)
                    pe.wait_ge(S["normed"], BASE + it + 1)
                    pe.wait_ge(S["p_copied"], BASE + 3 * it)
                    hold(pe, S["held_t"])
                    for n in range(KT + 1):
                        o = n * R if n < PB else 512 + (n - PB) * R
                        mm = nc.tensor.transpose(pp[:width[n], o:o + R], prob[p][:, at(n):at(n) + width[n]], con["ident"][:R, :R])
                    mm.then_inc(S["p_turned"], 1)
                    pe.wait_ge(S["p_copied"], BASE + 3 * it + 3)
                    pe.wait_ge(S["gathered"], BASE + it + 2)
                    for pr in range(3):
                        for n in range(KT + 1):
                            mm = nc.tensor.matmul(op[:2 * NT, pr * P:(pr + 1) * P], ptt[p][:width[n], n, pr * 2 * NT:(pr + 1) * 2 * NT],
                                                  vv[p][:width[n], n, pr * P:(pr + 1) * P], start=(n == 0), stop=(n == KT))
                    mm.then_inc(S["o_rows"], 1)
                    pe.wait_ge(S["rows_out"], BASE + it + 1)
                    hold(pe, S["held_t"])
                    for pr in range(3):
                        mm = nc.tensor.transpose(op[:, AW + pr * 2 * NT:AW + (pr + 1) * 2 * NT], orow[:, pr * P:(pr + 1) * P],
                                                 con["ident"][:2 * NT, :2 * NT])
                    mm.then_inc(S["o_sum"], 1)

                per_sample(pe, body)
                pe.wait_ge(S["gathered"], BASE + NB + 2)
                pe.wait_ge(S["copied_v"], BASE + EVEN * NB)
                for c in range(3):
                    mm = nc.tensor.transpose(tp[0][:NS, c * P:(c + 1) * P], ot[:, c, :], con["ident"][:, :])
                mm.then_inc(S["o_turned"], 1)


def project_out(nc, sem, io, con, mt, mb):
    KM = 3 * AW // P
    with ExitStack() as ctx:
        def sb(name, shape, dt=F32):
            return ctx.enter_context(nc.sbuf_tensor("o_" + name, shape, dt))

        two = lambda name, shape, dt=F32: [sb(f"{name}{p}", shape, dt) for p in range(2)]
        whi, wlo = sb("whi", [P, KM, D], F32R), sb("wlo", [P, KM, D], F32R)
        wraw = two("wraw", [P, D])
        xx, mm_, mbt = two("x", [P, D]), two("m", [P, 2 * AW]), two("mb", [P, 3, P])
        mf, mhi, mlo = two("mf", [P, KM * P]), two("mhi", [P, KM * P], F32R), two("mlo", [P, KM * P], F32R)
        yy, junk = two("y", [P, D]), sb("junk", [P, D])
        small = two("small", [P, 4])
        gfin = sb("gfin", [P, D])
        tp = [ctx.enter_context(nc.psum_tensor(f"o_t{b}", [P, 1024], F32)) for b in range(2)]
        yp = [ctx.enter_context(nc.psum_tensor(f"o_yp{b}", [P, 1024], F32)) for b in range(2)]
        ld = [sem(f"o_ld{p}") for p in range(2)]
        w_ld = [sem(f"o_w_ld{p}") for p in range(2)]
        x_ld = [sem(f"o_x_ld{p}") for p in range(2)]
        st_ = [sem(f"o_store{p}") for p in range(2)]
        S = {n: sem("o_" + n) for n in ("g_in", "w_hi", "w_lo", "turned", "copied", "hi", "lo", "y_sum", "resid", "square",
                                        "mean", "rstd", "scaled", "out")}

        def load_mixed(sp, p, t0, n):
            sp.dma_start(mm_[p][:n, :], mt[t0, :]).then_inc(ld[p], 16)
            sp.dma_start(mbt[p][:, :, :n], mb[:, t0].rearrange("(k p) t -> p k t", p=P)).then_inc(ld[p], 16)

        def staggered(eng, early, late):
            early(0, 0, 0, P)
            with eng.Fori(0, NTILE // 2 - 1) as i:
                for p in range(2):
                    early(2 * i + p + 1, i + p, 1 - p, P)
                    late(2 * i + p, i, p, P)
            for it in (NTILE - 2, NTILE - 1):
                early(it + 1, (it + 1) // 2, (it + 1) % 2, P if it + 1 < NTILE else NS)
                late(it, it // 2, it % 2, P)
            late(NTILE, NTILE // 2, 0, NS)

        with nc.Block() as block:
            @block.sync
            def _(sp):
                for p in range(2):
                    load_mixed(sp, p, slice(p * P, (p + 1) * P), P)
                    sp.dma_start(xx[p][:], io["xp"][p * P:(p + 1) * P, :]).then_inc(x_ld[p], 16)
                sp.dma_start(gfin[:], io["final_norm_g"].partition_broadcast(P)).then_inc(S["g_in"], 16)
                for k in range(KM):
                    if k >= 2:
                        sp.wait_ge(S["w_lo"], BASE + k - 1)
                    sp.dma_start(wraw[k % 2][:], io["w_out"][k * P:(k + 1) * P, :]).then_inc(w_ld[k % 2], 16)

                def more(it, p, n):
                    sp.wait_ge(S["lo"], BASE + it + 1)
                    load_mixed(sp, p, bass.ds((it + 2) * P, n), n)

                def done(it, p, n, x):
                    sp.wait_ge(S["out"], BASE + it + 3)
                    y = io["y_prompt"][bass.ds(it * P, P), :] if n == P else io["y_sample"]
                    sp.dma_start(y, yy[p][:n, :]).then_inc(st_[p], 16)
                    if x is not None:
                        sp.dma_start(xx[p][:x.shape[0], :], x).then_inc(x_ld[p], 16)

                more(0, 0, P)
                with sp.Fori(1, NTILE // 2 - 1) as i:
                    for p in range(2):
                        more(2 * i - 1 + p, 1 - p, P)
                        done(2 * i - 2 + p, p, P, io["xp"][bass.ds((2 * i + p) * P, P), :])
                more(NTILE - 3, 1, P)
                done(NTILE - 4, 0, P, io["xp"][(NTILE - 2) * P:(NTILE - 1) * P, :])
                more(NTILE - 2, 0, NS)
                done(NTILE - 3, 1, P, io["xp"][(NTILE - 1) * P:, :])
                done(NTILE - 2, 0, P, io["xs"])
                done(NTILE - 1, 1, P, None)
                done(NTILE, 0, NS, None)
                sp.wait_ge(st_[0], BASE + 16 * (NTILE // 2 + 1))
                sp.wait_ge(st_[1], BASE + 16 * (NTILE // 2))

            @block.gpsimd
            def _(pool):
                def tile(it, i, p, n):
                    pool.wait_ge(S["mean"], BASE + it + 1)
                    nc.gpsimd.tensor_tensor(small[p][:n, 2:3], small[p][:n, 1:2], con["mhalf"][:n, 0:1], ALU.pow).then_inc(S["rstd"], 1)

                with pool.Fori(0, NTILE // 2) as i:
                    for p in range(2):
                        tile(2 * i + p, i, p, P)
                tile(NTILE, NTILE // 2, 0, NS)

            @block.scalar
            def _(act):
                A = nc.scalar.activation

                def copy(it, i, p, n):
                    act.wait_ge(S["turned"], BASE + it + 1)
                    if not (isinstance(it, int) and it < 2):
                        act.wait_ge(S["lo"], BASE + it - 1)
                    for a, b, c in ((0, 3, 0), (6, 7, 3), (7, 9, 4)):
                        k3 = lambda t, a, b: t[:, a * P:b * P].rearrange("p (k t) -> p k t", t=P)[:, :, :n]
                        A(k3(mf[p], a, b), k3(tp[p], c, c + b - a), ACT.Copy).then_inc(S["copied"], 1)

                def square(it, i, p, n):
                    act.wait_ge(S["resid"], BASE + 2 * it + 2)
                    A(junk[:n, :], yy[p][:n, :], ACT.Square, accum_out=small[p][:n, 0:1]).then_inc(S["square"], 1)

                staggered(act, copy, square)

            @block.vector
            def _(dve):
                V = nc.vector
                dve.sem_inc(S["out"], 2)
                for k in range(KM):
                    dve.wait_ge(w_ld[k % 2], BASE + 16 * (k // 2 + 1))
                    V.tensor_copy(whi[:, k, :], wraw[k % 2][:]).then_inc(S["w_hi"], 1)
                    dve.wait_ge(S["w_hi"], BASE + k + 1)
                    V.tensor_tensor(wlo[:, k, :], wraw[k % 2][:], whi[:, k, :], ALU.subtract).then_inc(S["w_lo"], 1)
                dve.wait_ge(S["g_in"], BASE + 16)

                def split(it, i, p, n):
                    k3 = lambda t, a, b: t[:, a * P:b * P].rearrange("p (k t) -> p k t", t=P)[:, :, :n]
                    dve.wait_ge(ld[p], BASE + 32 * i + 32)
                    dve.wait_ge(S["copied"], BASE + 3 * it + 3)
                    if not (isinstance(it, int) and it < 2):
                        dve.wait_ge(S["y_sum"], BASE + it - 1)
                    parts = [(k3(mf[p], 0, 3), 0, 3), (mbt[p][:, :, :n], 3, 6), (k3(mf[p], 6, 9), 6, 9)]
                    for src, a, b in parts:
                        V.tensor_copy(k3(mhi[p], a, b), src).then_inc(S["hi"], 1)
                    for m, (src, a, b) in enumerate(parts):
                        dve.wait_ge(S["hi"], BASE + 3 * it + m + 1)
                        ins = V.tensor_tensor(k3(mlo[p], a, b), src, k3(mhi[p], a, b), ALU.subtract)
                    ins.then_inc(S["lo"], 1)

                def finish(it, i, p, n):
                    dve.wait_ge(S["y_sum"], BASE + it + 1)
                    dve.wait_ge(st_[p], BASE + 16 * i)
                    dve.wait_ge(x_ld[p], BASE + 16 * i + 16)
                    for h in range(2):
                        c = slice(h * 512, (h + 1) * 512)
                        V.tensor_tensor(yy[p][:n, c], yp[p][:n, c], xx[p][:n, c], ALU.add).then_inc(S["resid"], 1)
                    dve.wait_ge(S["square"], BASE + it + 1)
                    V.tensor_scalar(small[p][:n, 1:2], small[p][:n, 0:1], 1.0 / D, EPS, ALU.mult, ALU.add).then_inc(S["mean"], 1)
                    dve.wait_ge(S["rstd"], BASE + it + 1)
                    V.scalar_tensor_tensor(out=yy[p][:n, :], in0=yy[p][:n, :], scalar=small[p][:n, 2:3], in1=gfin[:n, :],
                                           op0=ALU.mult, op1=ALU.mult).then_inc(S["out"], 1)

                staggered(dve, split, finish)

            @block.tensor
            def _(pe):
                def turn(it, i, p, n):
                    pe.wait_ge(ld[p], BASE + 32 * i + 32)
                    if not (isinstance(it, int) and it < 2):
                        pe.wait_ge(S["copied"], BASE + 3 * it - 3)
                    for k in range(6):
                        t = nc.tensor.transpose(tp[p][:, k * P:k * P + n], mm_[p][:n, k * P:(k + 1) * P], con["ident"][:n, :n])
                    t.then_inc(S["turned"], 1)

                def product(it, i, p, n):
                    pe.wait_ge(S["lo"], BASE + it + 1)
                    pe.wait_ge(S["out"], BASE + it + 1)
                    for h in range(2):
                        for k in range(KM):
                            c = slice(h * 512, (h + 1) * 512)
                            a = slice(k * P, k * P + n)
                            y = mm3(nc, yp[p][:n, c], mhi[p][:, a], mlo[p][:, a], whi[:, k, c], wlo[:, k, c], k == 0, k == KM - 1)
                    y.then_inc(S["y_sum"], 1)

                pe.wait_ge(S["w_lo"], BASE + KM)
                staggered(pe, turn, product)


@contextmanager
def semaphores(nc):
    before = nc.snapshot_sems()

    def sem(name):
        made = nc.alloc_semaphore(name=name)
        nc.sync.sem_inc(made, BASE)
        return made

    yield sem
    nc.clear_and_free_semaphores(nc.allocated_since(before))
    nc.all_engine_barrier()


def build(nc, io, upto=99):
    with ExitStack() as ctx:
        scratch = lambda n, sh: io[n] if n in io else nc.dram_tensor(n, sh, F32, kind=io.get("scratch", "Internal")).ap()
        zf = scratch("zf", (NF * P, T))
        zt = scratch("zt", (T, TCOLS))
        mb = scratch("mb", (AW, T))
        mt = scratch("mt", (T, 2 * AW))
        con = {
            "ident": ctx.enter_context(nc.sbuf_tensor("c_ident", [P, P], F32)),
            "one": ctx.enter_context(nc.sbuf_tensor("c_one", [P, P], F32)),
            "mhalf": ctx.enter_context(nc.sbuf_tensor("c_mhalf", [P, 1], F32)),
        }
        with semaphores(nc) as sem:
            constants(nc, sem, con)
        if upto in (1, 99):
            with ExitStack() as stage, semaphores(nc) as sem:
                ht = [stage.enter_context(nc.sbuf_tensor(f"ht{p}", [P, KD, T], F32R)) for p in range(2)]
                norm_and_turn(nc, sem, None, io, con, ht)
                project(nc, sem, io, ht, zf, zt)
        if upto in (2, 99):
            with semaphores(nc) as sem:
                lru(nc, sem, io, con, zf, mb)
        if upto in (3, 99):
            with semaphores(nc) as sem:
                hgrn(nc, sem, io, con, zf, zt, mt)
        if upto in (4, 99):
            with semaphores(nc) as sem:
                attend_prompt(nc, sem, io, con, zf, zt, mt)
        if upto in (5, 99):
            with semaphores(nc) as sem:
                attend_sample(nc, sem, io, con, zf, zt, mt)
        if upto in (6, 99):
            with semaphores(nc) as sem:
                project_out(nc, sem, io, con, mt, mb)


_INS = {
    "x_prompt": ("xp", (SEQ, D)), "x_sample": ("xs", (NS, D)),
    "cache_k_win": ("ck", (NB, WIN, AW)), "cache_v_win": ("cv", (NB, WIN, AW)),
    "state_conv": ("state_conv", None), "state_lru": ("state_lru", None), "state_hgrn": ("state_hgrn", (NB, NH, P, HD)),
    "norm_g": ("norm_g", None), "w_in": ("w_in", (D, IN_W)), "conv_w": ("conv_w", None), "conv_b": ("conv_b", None),
    "lru_w_a": ("lru_w_a", None), "lru_b_a": ("lru_b_a", None), "lru_w_x": ("lru_w_x", None), "lru_b_x": ("lru_b_x", None),
    "lru_lambda": ("lru_lambda", None), "hgrn_lb_logits": ("hgrn_lb_logits", None), "hgrn_norm_g": ("hgrn_norm_g", None),
    "w_out": ("w_out", (3 * AW, D)), "final_norm_g": ("final_norm_g", None),
}
_OUTS = [
    ("y_prompt", (SEQ, D), (1, SEQ, D)), ("y_sample", (NS, D), (NB, NT, D)),
    ("k_win_prompt", (SEQ, AW), (1, 1, SEQ, NH, HD)), ("v_win_prompt", (SEQ, AW), (1, 1, SEQ, NH, HD)),
    ("k_win_sample", (NS, AW), (1, NB, NT, NH, HD)), ("v_win_sample", (NS, AW), (1, NB, NT, NH, HD)),
    ("conv_prompt", (1, 3, AW), (1, 1, 3, AW)), ("conv_sample", (NB, 3, AW), (1, NB, 3, AW)),
    ("lru_prompt", (1, AW), (1, 1, AW)), ("lru_sample", (NB, AW), (1, NB, AW)),
    ("hgrn_prompt", (1, NH, P, HD), (1, 1, NH, P, HD)), ("hgrn_sample", (NB, NH, P, HD), (1, NB, NH, P, HD)),
]


def kernel(**inputs):
    import numpy as _np
    import concourse.bacc as _bacc
    from concourse import mybir as _mybir
    from concourse.bass_utils import run_bass_kernel_spmd as _run

    nc = _bacc.Bacc("TRN2", target_bir_lowering=False, num_devices=1)
    arrays, io = {}, {}
    for name, (own, shape) in _INS.items():
        a = _np.ascontiguousarray(inputs[name])
        if shape is not None:
            a = a.reshape(shape)
        arrays[f"in_{own}"] = a
        io[own] = nc.dram_tensor(f"in_{own}", a.shape, _mybir.dt.from_np(a.dtype), kind="ExternalInput").ap()
    for own, shape, _ in _OUTS:
        io[own] = nc.dram_tensor(f"out_{own}", shape, _mybir.dt.float32, kind="ExternalOutput").ap()
    build(nc, io)
    r = _run(nc, [arrays], core_ids=[0])
    return tuple(r.results[0][f"out_{own}"].reshape(shape) for own, _, shape in _OUTS)
```
